# Optimizing a Trainium2 kernel written in Bass

```python
import math
import jax
import jax.numpy as jnp
from jax import lax
import numpy as np

D_MODEL = 1024
BATCH = 1
SEQ = 512
DEPTH = 1
DEC_BATCH = 8
DEC_SEQ = 16
PAST_LEN = 256

CHUNK = 64
Q_BLOCK = 128
EPS = 1e-6
FOX_HEADS = 8
FOX_HEAD_DIM = 128
FOX_WIDTH = FOX_HEADS * FOX_HEAD_DIM
FOX_FORGET_BIAS = 3.0
LRU_WIDTH = 1024
LRU_BLOCKS = 8
LRU_BLOCK_DIM = LRU_WIDTH // LRU_BLOCKS
CONV_WIDTH = 4
LRU_C = 8.0
GLA_HEADS = 4
GLA_DK = 128
GLA_DV = 256
GLA_QK_WIDTH = GLA_HEADS * GLA_DK
GLA_V_WIDTH = GLA_HEADS * GLA_DV
GLA_RANK = 16
GLA_TAU = 16.0
GLA_CHUNK = CHUNK
N_BRANCH = 3
BRANCH_WIDTH = 1024
D_FF = 4 * D_MODEL

SPLIT_SIZES = (FOX_WIDTH, FOX_WIDTH, FOX_WIDTH, FOX_HEADS,
               LRU_WIDTH, LRU_WIDTH,
               GLA_QK_WIDTH, GLA_QK_WIDTH, GLA_V_WIDTH, GLA_RANK, GLA_V_WIDTH,
               N_BRANCH * D_MODEL)
D_IN = FOX_WIDTH * 3 + FOX_HEADS + LRU_WIDTH * 2 + GLA_QK_WIDTH * 2 + GLA_V_WIDTH * 2 + GLA_RANK + N_BRANCH * D_MODEL

kernel_name = "hybrid_fox_rglru_gla_stream_step"

def _split_points():
    pts, acc = [], 0
    for s in SPLIT_SIZES[:-1]:
        acc += s
        pts.append(acc)
    return pts

def rms_norm(x, g):
    xf = x.astype(jnp.float32)
    y = xf * lax.rsqrt(jnp.mean(xf * xf, axis=-1, keepdims=True) + EPS)
    return (y * g.astype(jnp.float32)).astype(x.dtype)

def fox_attend(q, k, v, cq, ck, q_pos, k_pos):
    s = jnp.einsum('bqhd,bkhd->bhqk', q, k).astype(jnp.float32) * (FOX_HEAD_DIM ** -0.5)
    s = s + jnp.swapaxes(cq, 1, 2)[..., :, None] - jnp.swapaxes(ck, 1, 2)[..., None, :]
    mask = k_pos[None, :] <= q_pos[:, None]
    s = jnp.where(mask, s, -jnp.inf)
    p = jax.nn.softmax(s, axis=-1)
    return jnp.einsum('bhqk,bkhd->bqhd', p.astype(v.dtype), v)

def fox_prompt(q, k, v, c):
    B, T, H, Dh = q.shape
    nb = T // Q_BLOCK
    qb = q.reshape(B, nb, Q_BLOCK, H, Dh).swapaxes(0, 1)
    cb = c.reshape(B, nb, Q_BLOCK, H).swapaxes(0, 1)
    k_pos = jnp.arange(T)

    def block(args):
        i, qi, ci = args
        q_pos = i * Q_BLOCK + jnp.arange(Q_BLOCK)
        return fox_attend(qi, k, v, ci, c, q_pos, k_pos)

    o = lax.map(block, (jnp.arange(nb), qb, cb))
    return o.swapaxes(0, 1).reshape(B, T, H, Dh)

def causal_conv(x, buf, w, b):
    T = x.shape[1]
    xp = jnp.concatenate([buf, x], axis=1)
    y = b + sum(xp[:, j:j + T] * w[j] for j in range(CONV_WIDTH))
    return y, xp[:, -(CONV_WIDTH - 1):]

def rg_lru(x, h0, w_a, b_a, w_x, b_x, lam):
    B, T, W = x.shape
    xb = x.reshape(B, T, LRU_BLOCKS, LRU_BLOCK_DIM)
    r = jax.nn.sigmoid((jnp.einsum('btni,nij->btnj', xb, w_a).reshape(B, T, W) + b_a).astype(jnp.float32))
    i = jax.nn.sigmoid((jnp.einsum('btni,nij->btnj', xb, w_x).reshape(B, T, W) + b_x).astype(jnp.float32))
    log_a = LRU_C * r * jax.nn.log_sigmoid(lam.astype(jnp.float32))
    a = jnp.exp(log_a)
    mult = jnp.sqrt(-jnp.expm1(2.0 * log_a))
    u = mult * i * x.astype(jnp.float32)
    u = u.at[:, 0].add(a[:, 0] * h0)

    def combine(left, right):
        a1, b1 = left
        a2, b2 = right
        return a1 * a2, a2 * b1 + b2

    _, h = lax.associative_scan(combine, (a, u), axis=1)
    return h, h[:, -1]

def gla_chunked(q, k, v, log_a, S0):
    B, T, H, DK = q.shape
    DV = v.shape[-1]
    C = min(GLA_CHUNK, T)
    n = T // C
    f32 = jnp.float32
    qc = (q.astype(f32) * (DK ** -0.5)).reshape(B, n, C, H, DK)
    kc = k.astype(f32).reshape(B, n, C, H, DK)
    vc = v.astype(f32).reshape(B, n, C, H, DV)
    bcum = jnp.cumsum(log_a.reshape(B, n, C, H, DK), axis=2)
    b_last = bcum[:, :, -1:]
    q_t = qc * jnp.exp(bcum)
    k_t = kc * jnp.exp(-bcum)
    k_end = kc * jnp.exp(b_last - bcum)
    causal = jnp.tril(jnp.ones((C, C), dtype=bool))
    A = jnp.einsum('bnthd,bnshd->bnhts', q_t, k_t)
    A = jnp.where(causal, A, 0.0)
    o_intra = jnp.einsum('bnhts,bnshv->bnthv', A, vc)
    dS = jnp.einsum('bnshd,bnshv->bnhdv', k_end, vc)
    decay = jnp.exp(b_last[:, :, 0])

    def step(S, inp):
        dS_i, dec_i = inp
        return dec_i[..., None] * S + dS_i, S

    S_final, S_starts = lax.scan(step, S0, (jnp.moveaxis(dS, 1, 0), jnp.moveaxis(decay, 1, 0)))
    S_starts = jnp.moveaxis(S_starts, 0, 1)
    o_inter = jnp.einsum('bnthd,bnhdv->bnthv', q_t, S_starts)
    return (o_intra + o_inter).reshape(B, T, H, DV), S_final

def _layer(x, p, past):
    B, T, _ = x.shape
    f32 = jnp.float32
    xn = rms_norm(x, p['norm_mix_pre'])
    z = xn @ p['w_in']
    fq, fk, fv, ff, lx, lg, gq, gk, gv, glr, gog, mg = jnp.split(z, _split_points(), axis=-1)

    q = fq.reshape(B, T, FOX_HEADS, FOX_HEAD_DIM)
    k = fk.reshape(B, T, FOX_HEADS, FOX_HEAD_DIM)
    v = fv.reshape(B, T, FOX_HEADS, FOX_HEAD_DIM)
    logf = jax.nn.log_sigmoid((ff + p['b_fox_f']).astype(f32))
    if past is None:
        c = jnp.cumsum(logf, axis=1)
        o = fox_prompt(q, k, v, c)
        conv_buf = jnp.zeros((B, CONV_WIDTH - 1, LRU_WIDTH), x.dtype)
        h0 = jnp.zeros((B, LRU_WIDTH), f32)
        S0 = jnp.zeros((B, GLA_HEADS, GLA_DK, GLA_DV), f32)
    else:
        k_c, v_c, lf_c, conv_buf, h0, S0 = past
        P = k_c.shape[1]
        k_all = jnp.concatenate([k_c.astype(k.dtype), k], axis=1)
        v_all = jnp.concatenate([v_c.astype(v.dtype), v], axis=1)
        c_all = jnp.cumsum(jnp.concatenate([lf_c.astype(f32), logf], axis=1), axis=1)
        o = fox_attend(q, k_all, v_all, c_all[:, P:], c_all, P + jnp.arange(T), jnp.arange(P + T))
        conv_buf = conv_buf.astype(x.dtype)
        h0 = h0.astype(f32)
        S0 = S0.astype(f32)
    y_fox = o.reshape(B, T, FOX_WIDTH)

    xc, conv_new = causal_conv(lx, conv_buf, p['lru_conv_w'], p['lru_conv_b'])
    hseq, h_last = rg_lru(xc, h0, p['lru_w_a'], p['lru_b_a'], p['lru_w_x'], p['lru_b_x'], p['lru_lambda'])
    y_lru = jax.nn.gelu(lg) * hseq.astype(x.dtype)

    gqh = gq.reshape(B, T, GLA_HEADS, GLA_DK)
    gkh = gk.reshape(B, T, GLA_HEADS, GLA_DK)
    gvh = gv.reshape(B, T, GLA_HEADS, GLA_DV)
    gate_logit = (glr @ p['gla_w_gate_up'] + p['gla_b_gate']).astype(f32)
    log_a = (jax.nn.log_sigmoid(gate_logit) / GLA_TAU).reshape(B, T, GLA_HEADS, GLA_DK)
    o_gla, S_new = gla_chunked(gqh, gkh, gvh, log_a, S0)
    o_gla = rms_norm(o_gla, p['gla_norm']).astype(x.dtype).reshape(B, T, GLA_V_WIDTH)
    y_gla = o_gla * jax.nn.silu(gog)

    branches = jnp.stack([y_fox, y_lru, y_gla], axis=2)
    proj = jnp.einsum('btnc,ncd->btnd', branches, p['w_branch'])
    gates = jax.nn.sigmoid(mg).reshape(B, T, N_BRANCH, D_MODEL)
    mix = jnp.sum(gates * proj, axis=2) @ p['w_out']
    x = x + rms_norm(mix, p['norm_mix_post'])

    hn = rms_norm(x, p['norm_mlp_pre'])
    u = jnp.square(jax.nn.relu(hn @ p['w_up'])) @ p['w_down']
    x = x + rms_norm(u, p['norm_mlp_post'])
    new_state = (k, v, logf.astype(x.dtype), conv_new, h_last.astype(x.dtype), S_new.astype(x.dtype))
    return x, new_state

def setup_inputs(seed: int = 0) -> dict:
    key = jax.random.key(seed)
    ks = iter(jax.random.split(key, 32))
    f32 = jnp.float32

    def nrm(shape, scale=1.0):
        return scale * jax.random.normal(next(ks), shape, f32)

    x_prompt = nrm((BATCH, SEQ, D_MODEL))
    x_sample = nrm((DEC_BATCH, DEC_SEQ, D_MODEL))
    cache_fox_k = nrm((DEPTH, DEC_BATCH, PAST_LEN, FOX_HEADS, FOX_HEAD_DIM))
    cache_fox_v = nrm((DEPTH, DEC_BATCH, PAST_LEN, FOX_HEADS, FOX_HEAD_DIM))
    cache_fox_logf = jax.nn.log_sigmoid(FOX_FORGET_BIAS + nrm((DEPTH, DEC_BATCH, PAST_LEN, FOX_HEADS)))
    state_lru_conv = nrm((DEPTH, DEC_BATCH, CONV_WIDTH - 1, LRU_WIDTH))
    state_lru_h = nrm((DEPTH, DEC_BATCH, LRU_WIDTH), 0.5)
    state_gla = nrm((DEPTH, DEC_BATCH, GLA_HEADS, GLA_DK, GLA_DV), 2.0)
    norm_mix_pre = 1.0 + nrm((DEPTH, D_MODEL), 0.05)
    norm_mix_post = 1.0 + nrm((DEPTH, D_MODEL), 0.05)
    w_in = nrm((DEPTH, D_MODEL, D_IN), D_MODEL ** -0.5)
    b_fox_f = FOX_FORGET_BIAS + nrm((DEPTH, FOX_HEADS), 0.1)
    lru_conv_w = nrm((DEPTH, CONV_WIDTH, LRU_WIDTH), CONV_WIDTH ** -0.5)
    lru_conv_b = nrm((DEPTH, LRU_WIDTH), 0.02)
    lru_w_a = nrm((DEPTH, LRU_BLOCKS, LRU_BLOCK_DIM, LRU_BLOCK_DIM), LRU_BLOCK_DIM ** -0.5)
    lru_b_a = nrm((DEPTH, LRU_WIDTH), 0.02)
    lru_w_x = nrm((DEPTH, LRU_BLOCKS, LRU_BLOCK_DIM, LRU_BLOCK_DIM), LRU_BLOCK_DIM ** -0.5)
    lru_b_x = nrm((DEPTH, LRU_WIDTH), 0.02)
    u = jax.random.uniform(next(ks), (DEPTH, LRU_WIDTH), f32, 0.9, 0.999)
    s = u ** (1.0 / LRU_C)
    lru_lambda = jnp.log(s) - jnp.log1p(-s)
    gla_w_gate_up = nrm((DEPTH, GLA_RANK, GLA_QK_WIDTH), GLA_RANK ** -0.5)
    gla_b_gate = nrm((DEPTH, GLA_QK_WIDTH), 0.02)
    gla_norm = 1.0 + nrm((DEPTH, GLA_DV), 0.05)
    w_branch = nrm((DEPTH, N_BRANCH, BRANCH_WIDTH, D_MODEL), BRANCH_WIDTH ** -0.5)
    w_out = nrm((DEPTH, D_MODEL, D_MODEL), D_MODEL ** -0.5)
    norm_mlp_pre = 1.0 + nrm((DEPTH, D_MODEL), 0.05)
    norm_mlp_post = 1.0 + nrm((DEPTH, D_MODEL), 0.05)
    w_up = nrm((DEPTH, D_MODEL, D_FF), D_MODEL ** -0.5)
    w_down = nrm((DEPTH, D_FF, D_MODEL), D_FF ** -0.5)
    return {
        'x_prompt': x_prompt, 'x_sample': x_sample,
        'cache_fox_k': cache_fox_k, 'cache_fox_v': cache_fox_v, 'cache_fox_logf': cache_fox_logf,
        'state_lru_conv': state_lru_conv, 'state_lru_h': state_lru_h, 'state_gla': state_gla,
        'norm_mix_pre': norm_mix_pre, 'norm_mix_post': norm_mix_post, 'w_in': w_in, 'b_fox_f': b_fox_f,
        'lru_conv_w': lru_conv_w, 'lru_conv_b': lru_conv_b, 'lru_w_a': lru_w_a, 'lru_b_a': lru_b_a,
        'lru_w_x': lru_w_x, 'lru_b_x': lru_b_x, 'lru_lambda': lru_lambda,
        'gla_w_gate_up': gla_w_gate_up, 'gla_b_gate': gla_b_gate, 'gla_norm': gla_norm,
        'w_branch': w_branch, 'w_out': w_out, 'norm_mlp_pre': norm_mlp_pre, 'norm_mlp_post': norm_mlp_post,
        'w_up': w_up, 'w_down': w_down,
    }

def reference(x_prompt, x_sample, cache_fox_k, cache_fox_v, cache_fox_logf, state_lru_conv, state_lru_h,
              state_gla, norm_mix_pre, norm_mix_post, w_in, b_fox_f, lru_conv_w, lru_conv_b, lru_w_a, lru_b_a,
              lru_w_x, lru_b_x, lru_lambda, gla_w_gate_up, gla_b_gate, gla_norm, w_branch, w_out,
              norm_mlp_pre, norm_mlp_post, w_up, w_down):
    hp, hs = x_prompt, x_sample
    new_p = [[] for _ in range(6)]
    new_s = [[] for _ in range(6)]
    for l in range(DEPTH):
        p = {
            'norm_mix_pre': norm_mix_pre[l], 'norm_mix_post': norm_mix_post[l], 'w_in': w_in[l],
            'b_fox_f': b_fox_f[l], 'lru_conv_w': lru_conv_w[l], 'lru_conv_b': lru_conv_b[l],
            'lru_w_a': lru_w_a[l], 'lru_b_a': lru_b_a[l], 'lru_w_x': lru_w_x[l], 'lru_b_x': lru_b_x[l],
            'lru_lambda': lru_lambda[l], 'gla_w_gate_up': gla_w_gate_up[l], 'gla_b_gate': gla_b_gate[l],
            'gla_norm': gla_norm[l], 'w_branch': w_branch[l], 'w_out': w_out[l],
            'norm_mlp_pre': norm_mlp_pre[l], 'norm_mlp_post': norm_mlp_post[l],
            'w_up': w_up[l], 'w_down': w_down[l],
        }
        hp, st_p = _layer(hp, p, None)
        past = (cache_fox_k[l], cache_fox_v[l], cache_fox_logf[l], state_lru_conv[l], state_lru_h[l], state_gla[l])
        hs, st_s = _layer(hs, p, past)
        for lst, a in zip(new_p, st_p):
            lst.append(a)
        for lst, a in zip(new_s, st_s):
            lst.append(a)
    fox_k_p, fox_v_p, fox_lf_p, lru_conv_p, lru_h_p, gla_s_p = [jnp.stack(a) for a in new_p]
    fox_k_s, fox_v_s, fox_lf_s, lru_conv_s, lru_h_s, gla_s_s = [jnp.stack(a) for a in new_s]
    return (hp, hs, fox_k_p, fox_v_p, fox_lf_p, lru_conv_p, lru_h_p, gla_s_p,
            fox_k_s, fox_v_s, fox_lf_s, lru_conv_s, lru_h_s, gla_s_s)


_drawn_inputs = setup_inputs


def setup_inputs(seed=0):
    import zlib

    import numpy as np

    out = dict(_drawn_inputs(seed))
    spreads = {}
    factors = {'lru_b_a': 8.0, 'lru_b_x': 8.0, 'gla_b_gate': 6.662}
    for name, (base, spread) in spreads.items():
        noise = np.random.default_rng([zlib.crc32(name.encode()), seed]).standard_normal(out[name].shape)
        drawn = base * np.exp(spread * noise) if base else spread * noise
        out[name] = jnp.asarray(drawn.astype(out[name].dtype))
    for name, factor in factors.items():
        out[name] = (out[name] * factor).astype(out[name].dtype)
    return out
```

```python
from contextlib import ExitStack, contextmanager

import concourse.bass as bass
from concourse import mybir

ALU = mybir.AluOpType
ACT = mybir.ActivationFunctionType
AX = mybir.AxisListType
F32 = mybir.dt.float32
F32R = mybir.dt.float32r
BF16 = mybir.dt.bfloat16

P = 128
NEG = -1.0e30
ARENA = 22600
EPS = 1e-6
FOX_HEADS, FOX_DH = 8, 128
LRU_N, CONV_W, LRU_C = 8, 4, 8.0
GLA_H, GLA_DK, GLA_DV, GLA_RANK, GLA_TAU, GLA_CH = 4, 128, 256, 16, 16.0, 64
GELU_A, GELU_B = 0.7978845608028654, 0.044715


class Lin:

    def __init__(self, c, *terms):
        self.c, self.terms = c, terms

    def __add__(self, k):
        return Lin(self.c + k, *self.terms)

    def __mul__(self, k):
        return Lin(self.c * k, *[(m * k, r) for m, r in self.terms])

    def half(self):
        return Lin(self.c // 2, *[(m // 2, r) for m, r in self.terms])

    def loop(self, per, reg):
        return Lin(self.c, *self.terms, (per, reg))

    @property
    def v(self):
        out = self.c
        for m, r in self.terms:
            out = r * m + out
        return out

    def ds(self, size=1, scale=1, off=0):
        return bass.ds((self * scale + off).v, size)


class Steps:

    def __init__(self, eng, sem):
        self.eng, self.sem, self.at = eng, sem, Lin(0)

    def __call__(self, ins):
        ins.then_inc(self.sem, 1)
        self.at = self.at + 1
        self.eng.wait_ge(self.sem, self.at.v)

    @contextmanager
    def loop(self, n, per):
        start = self.at
        with self.eng.Fori(0, n) as i:
            self.at = start.loop(per, i)
            yield i
            assert self.at.c - start.c == per, f"{self.sem.name}: {self.at.c - start.c} steps, not {per}"
        self.at = start + n * per


def build(nc, ins, outs):
    (x_prompt, x_sample, cache_k, cache_v, cache_lf, st_conv, st_h, st_gla, n_mix_pre, n_mix_post,
     w_in, b_fox, conv_w, conv_b, lru_wa, lru_ba, lru_wx, lru_bx, lru_lam, gla_up, gla_bg,
     gla_norm, w_branch, w_out, n_mlp_pre, n_mlp_post, w_up, w_down) = ins
    (y_p, y_s, fk_p, fv_p, flf_p, lc_p, lh_p, gs_p, fk_s, fv_s, flf_s, lc_s, lh_s, gs_s) = outs

    TP, D = x_prompt.shape[1], x_prompt.shape[2]
    NB, TS_ = x_sample.shape[0], x_sample.shape[1]
    T = TP + NB * TS_
    HT = T // 2
    NT = T // P
    NTP = TP // P
    KT = D // P
    PAST = cache_k.shape[2]
    FF = w_up.shape[2]
    NG = FF // D
    assert T == NT * P and NB * TS_ == P and PAST == 2 * P and D == 1024 and HT <= 512

    cq, ck, cv, cff = 0, D, 2 * D, 3 * D
    clx = cff + FOX_HEADS
    clg = clx + D
    cgq = clg + D
    cgk = cgq + GLA_H * GLA_DK
    cgv = cgk + GLA_H * GLA_DK
    clr = cgv + GLA_H * GLA_DV
    cgo = clr + GLA_RANK
    cmg = cgo + GLA_H * GLA_DV

    B_FOX = 1
    B_MG = [0, 0, 0]
    B_MG[0] = B_FOX + 3 * FOX_HEADS
    B_LRU = B_MG[0] + 2 * KT
    B_MG[1] = B_LRU + 2 * LRU_N
    B_GLA = B_MG[1] + 2 * KT
    B_MG[2] = B_GLA + 6 * GLA_H
    B_OUT = B_MG[2] + 2 * KT
    B_MLP = B_OUT + KT
    N_BLK = B_MLP + NG * 2 * KT

    R_CONV0, R_H0, R_CW, R_CB, R_BA, R_BX, R_LAM, R_BG, R_GN = 0, 24, 32, 36, 37, 38, 39, 40, 41
    NR = 42

    w_in_v = w_in[0].rearrange("(k p) n -> p k n", p=P)
    w_br_v = [w_branch[0, r].rearrange("(k p) n -> p k n", p=P) for r in range(3)]
    w_out_v = w_out[0].rearrange("(k p) n -> p k n", p=P)
    w_up_v = w_up[0].rearrange("(k p) n -> p k n", p=P)
    w_dn_v = w_down[0].rearrange("(g k p) n -> g p k n", p=P, k=KT)

    with ExitStack() as ctx:
        def sb(name, shape, dt=F32):
            return ctx.enter_context(nc.sbuf_tensor(name, shape, dt))

        def sem(name):
            return ctx.enter_context(nc.semaphore(name))

        psum = ctx.enter_context(nc.psum_tensor("psum", [P, 8, 512], F32))
        bank = [psum[:, i, :] for i in range(8)]
        Z = bank[0:2]
        SBK = bank[2:4]
        TBK = bank[4:7]
        OBK = bank[7]

        XH = sb("XH", [P, KT, T], F32R)
        XL = sb("XL", [P, KT, T], F32R)
        YH = sb("YH", [P, KT, T], F32R)
        YL = sb("YL", [P, KT, T], F32R)
        raw = [sb(f"w_raw{s}", [P, KT, P]) for s in range(2)]
        WH = [sb(f"w_hi{s}", [P, KT, P], F32R) for s in range(2)]
        WL = [sb(f"w_lo{s}", [P, KT, P], F32R) for s in range(2)]
        idf = sb("ident", [P, P])
        idb = sb("ident_bf", [P, P], BF16)
        mask_p = sb("mask_prompt", [P, P], BF16)
        mask_s = sb("mask_sample", [P, P], BF16)
        gmask_p = sb("gmask_prompt", [P, P])
        gmask_s = sb("gmask_sample", [P, P])
        bmask = sb("bmask", [P, NB])
        col = sb("col", [P, KT, NR])
        lru_c4 = sb("lru_c4", [P, 2, LRU_N])
        bcol = sb("b_fox_col", [FOX_HEADS, 1])
        glr = sb("glr", [GLA_RANK, T])
        cn = sb("c_nat", [P, NT, FOX_HEADS])
        small = sb("small", [P, 12, 8])
        eps = sb("eps", [P, 1])
        fix = sb("fix", [P, NB, 1])
        last = sb("last", [P, LRU_N, 36])
        arena = sb("arena", [P, ARENA])

        def carve(start, *shapes):
            out, at = [], start
            for shape in shapes:
                n = 1
                for s in shape:
                    n *= s
                v = arena[:, at:at + n]
                if len(shape) == 2:
                    v = v.rearrange("p (a b) -> p a b", b=shape[1])
                if len(shape) == 3:
                    v = v.rearrange("p (a b c) -> p a b c", b=shape[1], c=shape[2])
                out.append(v)
                at += n
            assert at <= ARENA, at
            return out if len(out) > 1 else out[0]

        MIX = carve(0, (KT, T))
        A0 = KT * T

        nc_new = nc.dram_tensor("negc_new", (FOX_HEADS, T), F32, kind="Internal").ap()
        nc_past = nc.dram_tensor("negc_past", (FOX_HEADS, NB, PAST), F32, kind="Internal").ap()

        def sems(names):
            return [sem(n) for n in names.split()]

        raw_in = sems("raw_in0 raw_in1")
        w_hi, w_lo = sems("w_hi w_lo")
        z_done = sems("z_done0 z_done1")
        z_free = sems("z_free0 z_free1")
        dve_step, act_step, pool_step = sems("dve_step act_step pool_step")
        consts, pad_zero, pad_in, vec_in, lfc_in, g_rows, scr_out, stored = sems(
            "consts pad_zero pad_in vec_in lfc_in g_rows scr_out stored")
        eps_set, gla_init = sems("eps_set gla_init")
        x_in = [sem(f"x_in{t}") for t in range(NT)]
        root_done, hs_done, nt_done, nt_hi, nt_free = sems("root_done hs_done nt_done nt_hi nt_free")
        col_pe, col_sb, lam_ln, lru_cols = sems("col_pe col_sb lam_ln lru_cols")
        ff_ln, ff_lf, ff_c, cp_pe, cp_scan, cn_pe, lfn_pe, lfn_sb, cn_sb = sems(
            "ff_ln ff_lf ff_c cp_pe cp_scan cn_pe lfn_pe lfn_sb cn_sb")
        head_in = sems("head_in0 head_in1")
        kc_turned, kc_copied, kv_turned, kv_copied, kv_stored = sems(
            "kc_turned kc_copied kv_turned kv_copied kv_stored")
        qb_ready, s_done, s_read, m_ready, p_ready, p_turned, p_copied = sems(
            "qb_ready s_done s_read m_ready p_ready p_turned p_copied")
        o_done, on_ready, ot_turned, y_hi, y_done = sems("o_done on_ready ot_turned y_hi y_done")
        mix_sum = sem("mix_sum")
        wg_in, xc_ready, g_mm, r_act, a_act, m_dve, m_act, h_ready, yl_hi, yl_done = sems(
            "wg_in xc_ready g_mm r_act a_act m_dve m_act h_ready yl_hi yl_done")
        ge_sq, ge_dve, ge_act, ge_out, last_dve, last_pe, last_sb = sems(
            "ge_sq ge_dve ge_act ge_out last_dve last_pe last_sb")
        gu_in, s0_in, gs_stored, gg_mm, gg_act, gg_dve, ge3_act = sems(
            "gu_in s0_in gs_stored gg_mm gg_act gg_dve ge3_act")
        ke_ready, ke_turned, ken_ready, kem_ready, v_turned, v_copied, ds_done, ds_read = sems(
            "ke_ready ke_turned ken_ready kem_ready v_turned v_copied ds_done ds_read")
        q_ready, at_done, at_ready, go_done, go_read, go_root, go_ready = sems(
            "q_ready at_done at_ready go_done go_read go_root go_ready")
        sg_tanh, gt_turned, gt_copied, gy_dve, gy_hi, gy_done = sems(
            "sg_tanh gt_turned gt_copied gy_dve gy_hi gy_done")
        mix_hi, mix_split, nat_pe, nat_free, x_again, nat_root, x2_ready, x2_root = sems(
            "mix_hi mix_split nat_pe nat_free x_again nat_root x2_ready x2_root")
        u_sq, u_hi = sems("u_sq u_hi")
        u_done = sems("u_done0 u_done1")
        fin_ready = sem("fin_ready")

        XN = carve(0, (NT, D))
        HS0, vrow, junk, G0 = carve(A0, (2, D), (D,), (D,), (D,))
        cp_raw, cpast, rst_p, lfT, cT, ncT, rst_n, fz, lfn = carve(
            A0 + 10240 - 1024, (P,), (NB * PAST,), (NB * PAST,), (T,), (T,), (T,), (T,), (T,), (NT, FOX_HEADS))
        QT, KTt, VTt, KVN, KC0, KC1, VC0, VC1, CB, SP, PTB, ON = carve(
            A0, (2, T), (2, T), (2, T), (2 * NT, P), (2 * NB, P), (2 * NB, P), (2 * NB, P), (2 * NB, P),
            (2, 896), (2, 512), (2, 512), (2, P))
        KC, VC = (KC0, KC1), (VC0, VC1)
        KCT, PM, QB = carve(0, (2 * NB, P), (2, NB, P), (NB, P))
        GT, TMP = carve(ARENA - 2 * T, (T,), (T,))
        XPW = CONV_W - 1 + TP + NB * (CONV_W - 1 + TS_)
        (WG, LG, GQ, TG, Y2, RA, RX, AA, TH, A2, MM, UU, HH, XC, XP, LS) = carve(
            A0, (2, P), (T,), (T,), (T,), (T,), (T,), (T,), (T,), (T,), (T,), (T,), (T,), (T,), (T,), (XPW + 1,), (D,))
        XPS = XP[:, CONV_W - 1 + TP:XPW].rearrange("p (b t) -> p b t", b=NB)
        (QG, KG, KTl, ZG, BC, E1, E2, E3, KEM, VT2, VN, QGB, S0, SA, OS, RG, GU, SG) = carve(
            A0, (T,), (T,), (T,), (T,), (T,), (T,), (T,), (T,), (NB, P), (2, T), (NT, GLA_DV),
            (NB, P), (NB, GLA_DV), (TP // GLA_CH + 1, GLA_DV), (NT, GLA_DV), (T,), (P,), (2, T))
        AT = ZG.rearrange("p (a b) -> p a b", b=P)
        KEN = BC.rearrange("p (a b) -> p a b", b=P)
        OT = VT2
        OTB, X2, G1, G2, G3 = carve(A0, (KT, T), (NT, D), (D,), (D,), (D,))
        HS1, NJ, TM = carve(0, (2, D), (D,), (D,))
        UR, UQ = carve(A0, (T,), (T,))
        FN, FJ = carve(A0, (D,), (D,))

        blk = ctx.enter_context(nc.Block())

        def halves(v):
            return v[:, 0:HT], v[:, HT:T]

        def by_sample(v):
            return v[:, TP:T].rearrange("p (b t) -> p b t", t=TS_)

        def diag(v):
            return bass.AP(tensor=v.tensor, offset=v.offset, ap=[v.ap[0], [P + TS_, NB], [1, TS_]])

        def tok(t):
            return slice(t * P, (t + 1) * P)

        DS_PROMPT = ((2, (0, 2)), (4, (1, 3)), (3, (4, 6)), (5, (5, 7)))
        DS_SAMPLE = ((2, (0, 1)), (3, (2, 3)), (4, (4, 5)), (5, (6, 7)))
        ORD = (0, 1, 4, 2, 3)

        @blk.sync
        def _(sp):
            def load(b, s, src):
                if not (isinstance(b, Lin) and not b.terms and b.c < 2):
                    sp.wait_ge(w_lo, (b + -1).v)
                sp.dma_start(raw[s][:, :, :], src).then_inc(raw_in[s], 16)

            for t in range(NTP):
                sp.dma_start(XN[:, t, :], x_prompt[0, t * P:(t + 1) * P, :]).then_inc(x_in[t], 16)
            sp.dma_start(XN[:, NTP, :], x_sample.rearrange("b t d -> (b t) d")).then_inc(x_in[NTP], 16)
            sp.dma_start(G0[:, :], n_mix_pre[0:1, :].broadcast_to((P, D))).then_inc(g_rows, 16)
            sp.wait_ge(pad_zero, 2)
            sp.dma_start(raw[0][:, :, 0:FOX_HEADS], w_in_v[:, :, cff:cff + FOX_HEADS]).then_inc(raw_in[0], 16)
            sp.dma_start(raw[0][:, :, 32:32 + GLA_RANK], w_in_v[:, :, clr:clr + GLA_RANK]).then_inc(pad_in, 16)
            for r, v in ((R_CONV0, st_conv[0].rearrange("b j c -> (b j) c")), (R_H0, st_h[0]), (R_CW, conv_w[0]),
                         (R_CB, conv_b), (R_BA, lru_ba), (R_BX, lru_bx), (R_LAM, lru_lam)):
                sp.dma_start(vrow[r:r + v.shape[0], :], v).then_inc(vec_in, 16)
            sp.dma_start(vrow[R_BG:R_BG + 1, 0:GLA_H * GLA_DK], gla_bg).then_inc(vec_in, 16)
            sp.dma_start(vrow[R_GN:R_GN + 1, 0:GLA_DV], gla_norm).then_inc(vec_in, 16)
            sp.dma_start(bcol[:, :], b_fox.rearrange("o h -> h o")).then_inc(vec_in, 16)
            sp.dma_start(cp_raw[:, :], cache_lf[0].rearrange("b (q r) h -> (b q) (r h)", r=16)).then_inc(lfc_in, 16)

            def w_fox(h, part):
                return w_in_v[:, :, h.ds(P, P, part * D)] if h.terms else w_in_v[:, :, part * D + h.c * P:part * D + (h.c + 1) * P]

            def load_heads(h, par):
                hd = h.ds() if h.terms else slice(h.c, h.c + 1)
                for c, dst in ((cache_k, KC[par]), (cache_v, VC[par])):
                    sp.dma_start(dst[:, :, :], c[0].rearrange("b (f p) h d -> p (b f) h d", p=P)[:, :, hd, :]
                                 .rearrange("p f o d -> p f (o d)")).then_inc(head_in[par], 16)
                sp.dma_start(CB[:, par, 0:TP], nc_new[hd, 0:TP].broadcast_to((P, TP))).then_inc(head_in[par], 16)
                sp.dma_start(CB[:, par, TP:TP + PAST], nc_past[hd, :, :].rearrange("o b s -> (o b) s")
                             .unsqueeze(1).broadcast_to((NB, TS_, PAST))).then_inc(head_in[par], 16)
                sp.dma_start(CB[:, par, TP + PAST:], nc_new[hd, TP:T].broadcast_to((P, P))).then_inc(head_in[par], 16)

            def store_kv(a):
                hd = a.ds() if a.terms else slice(a.c, a.c + 1)
                sp.wait_ge(kv_copied, (a * 3 + 3).v)
                for dp, ds_, at in ((fv_p, fv_s, 0), (fk_p, fk_s, NT)):
                    sp.dma_start(dp[0, 0, :, hd, :].rearrange("(t p) o d -> p t (o d)", p=P),
                                 KVN[:, at:at + NTP, :]).then_inc(kv_stored, 16)
                    sp.dma_start(ds_[0, :, :, hd, :].rearrange("b t o d -> (b t) (o d)"),
                                 KVN[:, at + NTP, :]).then_inc(kv_stored, 16)

            def fox_window(a, par, proj):
                b = a * 3 + (B_FOX + 3)
                s = (B_FOX + 3 + par) % 2
                if proj:
                    load(b, s, w_fox(a + 1, 0))
                    load(b + 1, 1 - s, w_fox(a + 1, 1))
                    if a.terms or a.c > 0:
                        sp.wait_ge(o_done, (a * 5).v)
                    load_heads(a + 1, 1 - par)
                    load(b + 2, s, w_fox(a + 1, 2))
                store_kv(a)

            for part in range(2):
                load(Lin(B_FOX + part), (B_FOX + part) % 2, w_fox(Lin(0), part))
            sp.wait_ge(ff_c, 1)
            sp.dma_start(nc_new, ncT[0:FOX_HEADS, :]).then_inc(scr_out, 16)
            sp.wait_ge(cp_scan, 1)
            sp.dma_start(nc_past, cpast[0:FOX_HEADS, :].rearrange("h (b s) -> h b s", s=PAST)).then_inc(scr_out, 16)
            load(Lin(B_FOX + 2), (B_FOX + 2) % 2, w_fox(Lin(0), 2))
            sp.wait_ge(lfn_sb, 1)
            sp.dma_start(flf_p[0, 0].rearrange("(t p) h -> p t h", p=P), lfn[:, 0:NTP, :]).then_inc(stored, 16)
            sp.dma_start(flf_s[0].rearrange("b t h -> (b t) h"), lfn[:, NTP, :]).then_inc(stored, 16)
            sp.wait_ge(scr_out, 32)
            sp.wait_ge(cn_sb, 1)
            sp.wait_ge(stored, 32)
            load_heads(Lin(0), 0)
            fox_window(Lin(0), 0, True)
            with sp.Fori(0, FOX_HEADS // 2 - 1) as i:
                fox_window(Lin(1, (2, i)), 1, True)
                fox_window(Lin(2, (2, i)), 0, True)

            def merge_loads(r, j):
                b = Lin(B_MG[r]) + 2 * j.c if not j.terms else Lin(B_MG[r] + 2 * j.c, (2, j.terms[0][1]))
                load(b, B_MG[r] % 2, w_in_v[:, :, j.ds(P, P, cmg + r * D) if j.terms else slice(cmg + r * D, cmg + r * D + P)])
                load(b + 1, 1 - B_MG[r] % 2, w_br_v[r][:, :, j.ds(P, P) if j.terms else slice(0, P)])

            def merge(r):
                with sp.Fori(0, KT - 1) as i:
                    merge_loads(r, Lin(1, (1, i)))

            merge_loads(0, Lin(0))
            fox_window(Lin(FOX_HEADS - 1), 1, False)
            merge(0)

            def lru_loads(n, first=False):
                b = n * 2 + B_LRU
                c = (lambda c0: n.ds(P, P, c0) if n.terms else slice(c0 + n.c * P, c0 + (n.c + 1) * P))
                load(b, B_LRU % 2, w_in_v[:, :, c(clx)])
                load(b + 1, 1 - B_LRU % 2, w_in_v[:, :, c(clg)])
                if not first:
                    sp.wait_ge(g_mm, n.v)
                nd = n.ds() if n.terms else slice(n.c, n.c + 1)
                for i, w in enumerate((lru_wa, lru_wx)):
                    sp.dma_start(WG[:, i, :], w[0, nd].rearrange("n i j -> (n i) j")).then_inc(wg_in, 16)

            sp.wait_ge(y_done, 5 * FOX_HEADS)
            sp.wait_ge(kv_stored, 64 * FOX_HEADS)
            lru_loads(Lin(0), True)
            with sp.Fori(0, LRU_N - 1) as i:
                lru_loads(Lin(1, (1, i)))
            merge_loads(1, Lin(0))
            merge(1)
            load(Lin(B_GLA), B_GLA % 2, w_in_v[:, :, cgk:cgk + P])
            sp.wait_ge(last_sb, 1)
            sp.dma_start(lc_p[0, 0], LS[0:3, :]).then_inc(stored, 16)
            sp.dma_start(lc_s[0].rearrange("b j c -> (b j) c"), LS[3:27, :]).then_inc(stored, 16)
            sp.dma_start(lh_p[0], LS[27:28, :]).then_inc(stored, 16)
            sp.dma_start(lh_s[0], LS[28:36, :]).then_inc(stored, 16)
            sp.wait_ge(stored, 32 + 64)

            def gla_loads(h, first=False):
                b = h * 6 + B_GLA
                s = B_GLA % 2
                hd = h.ds() if h.terms else slice(h.c, h.c + 1)

                def c(c0, per, off=0):
                    return h.ds(P, per, c0 + off) if h.terms else slice(c0 + off + h.c * per, c0 + off + h.c * per + P)
                if not first:
                    load(b, s, w_in_v[:, :, c(cgk, P)])
                    store_states(h + -1)
                    sp.wait_ge(gg_mm, h.v)
                sp.dma_start(GU[0:GLA_RANK, :], gla_up[0][:, c(0, P)]).then_inc(gu_in, 16)
                load(b + 1, 1 - s, w_in_v[:, :, c(cgv, GLA_DV)])
                if not first:
                    sp.wait_ge(gs_stored, (h * 32).v)
                sp.dma_start(S0[:, :, :], st_gla[0][:, hd].rearrange("b o k v -> k b (o v)")).then_inc(s0_in, 16)
                load(b + 2, s, w_in_v[:, :, c(cgv, GLA_DV, P)])
                load(b + 3, 1 - s, w_in_v[:, :, c(cgq, P)])
                load(b + 4, s, w_in_v[:, :, c(cgo, GLA_DV)])
                load(b + 5, 1 - s, w_in_v[:, :, c(cgo, GLA_DV, P)])

            def store_states(h):
                hd = h.ds() if h.terms else slice(h.c, h.c + 1)
                sp.wait_ge(ds_read, (h * 8 + 8).v)
                sp.dma_start(gs_p[0, 0][hd].rearrange("o k v -> (o k) v"), SA[:, TP // GLA_CH, :]).then_inc(gs_stored, 16)
                sp.dma_start(gs_s[0][:, hd].rearrange("b o k v -> k b (o v)"), S0[:, :, :]).then_inc(gs_stored, 16)

            gla_loads(Lin(0), True)
            with sp.Fori(0, GLA_H - 1) as i:
                gla_loads(Lin(1, (1, i)))
            merge_loads(2, Lin(0))
            store_states(Lin(GLA_H - 1))
            merge(2)
            sp.wait_ge(gy_done, 2 * GLA_H)
            sp.wait_ge(gs_stored, 32 * GLA_H)
            for g, v in ((G1, n_mix_post), (G2, n_mlp_pre), (G3, n_mlp_post)):
                sp.dma_start(g[:, :], v[0:1, :].broadcast_to((P, D))).then_inc(x_again, 16)
            sp.dma_start(X2[:, 0:NTP, :], x_prompt[0].rearrange("(t p) d -> p t d", p=P)).then_inc(x_again, 16)
            sp.dma_start(X2[:, NTP, :], x_sample.rearrange("b t d -> (b t) d")).then_inc(x_again, 16)
            with sp.Fori(0, KT // 2) as i:
                for s in range(2):
                    load(Lin(B_OUT + s, (2, i)), (B_OUT + s) % 2, w_out_v[:, :, bass.ds(i * (2 * P) + s * P, P)])

            def up_loads(b, g, n):
                with sp.Fori(0, n) as j:
                    for s in range(2):
                        cols = j * (2 * P) + ((g * D + s * P) if isinstance(g, int) else g * D + s * P)
                        load(b.loop(2, j) + s, (B_MLP + s) % 2, w_up_v[:, :, bass.ds(cols, P)])

            def down_loads(b, g, n):
                with sp.Fori(0, n) as j:
                    for s in range(2):
                        w = w_dn_v[g] if isinstance(g, int) else w_dn_v[bass.ds(g, 1)].rearrange("o p k n -> (o p) k n")
                        load(b.loop(2, j) + s, (B_MLP + s) % 2, w[:, :, bass.ds(j * (2 * P) + s * P, P)])


            up_loads(Lin(B_MLP), 0, KT // 2)
            down_loads(Lin(B_MLP + KT), 0, KT // 2)
            with sp.Fori(1, NG) as g:
                up_loads(Lin(B_MLP, (2 * KT, g)), g, KT // 2)
                down_loads(Lin(B_MLP + KT, (2 * KT, g)), g, KT // 2)
            for t in range(NT):
                sp.wait_ge(fin_ready, t + 1)
                dst = y_p[0, t * P:(t + 1) * P, :] if t < NTP else y_s.rearrange("b t d -> (b t) d")
                sp.dma_start(dst, X2[:, t, :]).then_inc(stored, 16)
            sp.wait_ge(stored, 32 + 64 + 16 * NT)
            sp.wait_ge(kv_stored, 64 * FOX_HEADS)
            sp.wait_ge(gs_stored, 32 * GLA_H)
            sp.wait_ge(scr_out, 32)

        @blk.tensor
        def _(pe):
            def block(b, s, AH, AL, after=(None, None), a_ready=None):
                pe.wait_ge(w_lo, (b + 1).v)
                for h in range(2):
                    if b.terms or b.c > 0:
                        pe.wait_ge(z_free[h], b.v)
                    for k in range(KT):
                        if a_ready is not None:
                            a_ready(h, k)
                        for i, (w, x) in enumerate(((WH, AH), (WH, AL), (WL, AH))):
                            mm = pe.matmul(Z[h][:, 0:HT], w[s][:, k, :], x[:, k, h * HT:(h + 1) * HT],
                                           start=(k == 0 and i == 0), stop=(k == KT - 1 and i == 2))
                    mm.then_inc(z_done[h], 1)
                    if after[h] is not None:
                        after[h]()

            def norm_turn(n, t, HS):
                c = n * NT + t
                pe.wait_ge(hs_done, c + 1)
                for q in range(2):
                    bk = bank[(2 + 2 * (t % 2) if n == 0 else 6) + q]
                    back = 2 - n
                    if t >= back:
                        pe.wait_ge(nt_free, 2 * (c - back) + q + 1)
                    for k in range(4):
                        mm = pe.transpose(bk[:, k * P:(k + 1) * P], HS[:, t % 2, (4 * q + k) * P:(4 * q + k + 1) * P], idf[:, :])
                    mm.then_inc(nt_done, 1)

            pe.wait_ge(consts, 2)
            for t in range(NT):
                norm_turn(0, t, HS0)
            pe.wait_ge(vec_in, 16 * 10)
            for k in range(KT):
                mm = pe.transpose(bank[6][:, k * NR:(k + 1) * NR], vrow[0:NR, k * P:(k + 1) * P], idf[0:NR, 0:NR])
            mm.then_inc(col_pe, 1)
            pe.wait_ge(nt_free, 2 * NT)
            block(Lin(0), 0, XH, XL)
            pe.wait_ge(lfc_in, 16)
            for r in range(16):
                mm = pe.transpose(bank[2 + r // 4][0:FOX_HEADS, (r % 4) * P:(r % 4 + 1) * P],
                                  cp_raw[:, r * FOX_HEADS:(r + 1) * FOX_HEADS], idf[:, :])
                if r % 4 == 3:
                    mm.then_inc(cp_pe, 1)
            block(Lin(1), 1, XH, XL)
            pe.wait_ge(ff_lf, 1)
            pe.wait_ge(col_sb, 1)
            for t in range(NT):
                mm = pe.transpose(bank[6][:, t * 8:t * 8 + 8], lfT[0:FOX_HEADS, tok(t)], idf[0:FOX_HEADS, 0:FOX_HEADS])
            mm.then_inc(lfn_pe, 1)
            block(Lin(2), 0, XH, XL)
            pe.wait_ge(ff_c, 1)
            for t in range(NT):
                mm = pe.transpose(bank[7][:, t * 8:t * 8 + 8], cT[0:FOX_HEADS, tok(t)], idf[0:FOX_HEADS, 0:FOX_HEADS])
            mm.then_inc(cn_pe, 1)
            block(Lin(3), 1, XH, XL)

            pe.wait_ge(consts, 5)
            pe.wait_ge(cn_sb, 1)

            def fox_window(a, par, proj):
                b = a * 3 + (B_FOX + 3)
                s = (B_FOX + 3 + par) % 2
                some = bool(a.terms) or a.c > 0

                def turn_kc(j):
                    if j == 0:
                        pe.wait_ge(head_in[par], (a.half() * 80 + 80).v)
                        if some:
                            pe.wait_ge(kv_copied, (a * 3).v)
                    if j >= 2:
                        pe.wait_ge(kc_copied, (a * 4 + (j - 1)).v)
                    for i in range(4):
                        mm = pe.transpose(TBK[j % 2][:, i * P:(i + 1) * P], KC[par][:, 4 * j + i, :], idf[:, :])
                    mm.then_inc(kc_turned, 1)

                def turn_kv(j):
                    if j == 0:
                        pe.wait_ge(kc_copied, (a * 4 + 4).v)
                    if j == 2:
                        pe.wait_ge(kv_copied, (a * 3 + 1).v)
                    for i in range(4 * j, min(4 * j + 4, 2 * NT)):
                        src = VTt if i < NT else KTt
                        mm = pe.transpose(TBK[j % 2][:, (i - 4 * j) * P:(i - 4 * j + 1) * P], src[:, par, tok(i % NT)], idf[:, :])
                    mm.then_inc(kv_turned, 1)

                def scores(p):
                    t, S = ORD[p], SBK[p % 2]
                    if p == 0:
                        pe.wait_ge(z_free[0], b.v)
                        pe.wait_ge(z_free[1], b.v)
                    if p < 2:
                        if some:
                            pe.wait_ge(s_read, (a * 5).v)
                    else:
                        pe.wait_ge(s_read, (a * 5 + (p - 1)).v)
                    w, mask = (t + 1) * P, mask_p
                    if t == NTP:
                        pe.wait_ge(qb_ready, (a + 1).v)
                        pe.wait_ge(kc_copied, (a * 4 + 4).v)
                        for i in range(NB):
                            pe.matmul(S[:, 0:PAST], QB[:, i, :], KCT[:, 2 * i:2 * i + 2, :].rearrange("p a b -> p (a b)"),
                                      start=(i == 0), stop=(i == NB - 1))
                        w, mask = PAST + P, mask_s
                        pe.matmul(S[:, PAST:w], QT[:, par, TP:T], KTt[:, par, TP:T], start=True, stop=False)
                    else:
                        pe.matmul(S[:, 0:w], QT[:, par, tok(t)], KTt[:, par, 0:w], start=True, stop=False)
                    pe.matmul(S[:, w - P:w], idb[:, :], mask[:, :], start=False, stop=True).then_inc(s_done, 1)

                def turn_p(p):
                    t = ORD[p]
                    n = t + 1 if t < NTP else 3
                    pe.wait_ge(p_ready, (a * 5 + (p + 1)).v)
                    if some or p > 0:
                        pe.wait_ge(p_copied, (a * 5 + p).v)
                    for i in range(n):
                        mm = pe.transpose(TBK[2][:, i * P:(i + 1) * P], SP[:, p % 2, i * P:(i + 1) * P], idf[:, :])
                    mm.then_inc(p_turned, 1)

                def times_v(p):
                    t = ORD[p]
                    pe.wait_ge(p_copied, (a * 5 + (p + 1)).v)
                    pe.wait_ge(kv_copied, (a * 3 + min(p + 1, 3) if p else a * 3 + 1).v)
                    if some or p > 0:
                        pe.wait_ge(y_done, (a * 5 + p).v)
                    keys = range(t + 1) if t < NTP else [NTP]
                    pairs = [(PTB[:, p % 2, i * P:(i + 1) * P], KVN[:, key, :]) for i, key in enumerate(keys)]
                    if t == NTP:
                        pairs += [(PM[:, f, i, :], VC[par][:, 2 * i + f, :]) for i in range(NB) for f in range(2)]
                    for i, (w, x) in enumerate(pairs):
                        mm = pe.matmul(OBK[:, 0:P], w, x, start=(i == 0), stop=(i == len(pairs) - 1))
                    mm.then_inc(o_done, 1)

                def turn_o(p):
                    pe.wait_ge(on_ready, (a * 5 + (p + 1)).v)
                    pe.transpose(OBK[:, P:2 * P], ON[:, p % 2, :], idf[:, :]).then_inc(ot_turned, 1)

                def unit(*todo):
                    def run():
                        for f, x in todo:
                            f(x)
                    return run

                u = [unit((turn_kc, 0), (turn_kc, 1), (scores, 0), (scores, 1)),
                     unit((turn_kc, 2), (turn_kc, 3), (turn_p, 0), (turn_kv, 0)),
                     unit((scores, 2), (turn_p, 1), (times_v, 0), (turn_kv, 1), (turn_kv, 2)),
                     unit((turn_o, 0), (scores, 3), (turn_p, 2), (times_v, 1)),
                     unit((turn_o, 1), (scores, 4), (turn_p, 3), (times_v, 2)),
                     unit((turn_o, 2), (turn_p, 4), (times_v, 3), (turn_o, 3), (times_v, 4), (turn_o, 4))]
                if proj:
                    block(b, s, XH, XL, (u[0], u[1]))
                    block(b + 1, 1 - s, XH, XL, (u[2], u[3]))
                    block(b + 2, s, XH, XL, (u[4], u[5]))
                else:
                    for f in u:
                        f()

            fox_window(Lin(0), 0, True)
            with pe.Fori(0, FOX_HEADS // 2 - 1) as i:
                fox_window(Lin(1, (2, i)), 1, True)
                fox_window(Lin(2, (2, i)), 0, True)
            fox_window(Lin(FOX_HEADS - 1), 1, False)

            def merge(r, y_sem, y_count):
                s = B_MG[r] % 2
                with pe.Fori(0, KT) as j:
                    b = Lin(B_MG[r], (2, j))
                    block(b, s, XH, XL)
                    pe.wait_ge(y_sem, y_count)
                    block(b + 1, 1 - s, YH, YL)

            merge(0, y_done, 5 * FOX_HEADS)

            def lru_window(n):
                b = n * 2 + B_LRU

                def gates():
                    pe.wait_ge(xc_ready, (n + 1).v)
                    pe.wait_ge(wg_in, (n * 32 + 32).v)
                    if n.terms or n.c > 0:
                        pe.wait_ge(r_act, n.v)
                    for i in range(2):
                        for h in range(2):
                            mm = pe.matmul(bank[2 + 2 * i + h][:, 0:HT], WG[:, i, :], XC[:, h * HT:(h + 1) * HT],
                                           start=True, stop=True)
                    mm.then_inc(g_mm, 1)
                block(b, B_LRU % 2, XH, XL)
                block(b + 1, 1 - B_LRU % 2, XH, XL, (None, gates))

            lru_window(Lin(0))
            with pe.Fori(0, LRU_N - 1) as i:
                lru_window(Lin(1, (1, i)))
            merge(1, yl_done, LRU_N)
            pe.wait_ge(last_dve, 1)
            for n in range(LRU_N):
                mm = pe.transpose(bank[2 + n // 4][0:36, (n % 4) * P:(n % 4 + 1) * P], last[:, n, :], idf[:, :])
            mm.then_inc(last_pe, 1)

            def gla_head(h):
                b = h * 6 + B_GLA
                s = B_GLA % 2
                some = bool(h.terms) or h.c > 0

                def gate():
                    pe.wait_ge(gu_in, (h * 16 + 16).v)
                    if some:
                        pe.wait_ge(ds_read, (h * 8).v)
                        pe.wait_ge(at_ready, (h * 2).v)
                    else:
                        pe.wait_ge(last_sb, 1)
                    for q in range(2):
                        mm = pe.matmul(SBK[q][:, 0:HT], GU[0:GLA_RANK, :], glr[:, q * HT:(q + 1) * HT], start=True, stop=True)
                    mm.then_inc(gg_mm, 1)

                def turn_ke():
                    pe.wait_ge(ke_ready, (h + 1).v)
                    if some:
                        pe.wait_ge(gt_copied, (h * 3).v)
                    for t in range(NT):
                        mm = pe.transpose(TBK[t // 4][:, (t % 4) * P:(t % 4 + 1) * P], KG[:, tok(t)], idf[:, :])
                    mm.then_inc(ke_turned, 1)

                def turn_v():
                    pe.wait_ge(z_free[0], (b + 3).v)
                    pe.wait_ge(z_free[1], (b + 3).v)
                    pe.wait_ge(ken_ready, (h + 1).v)
                    for t in range(NT):
                        for e in range(2):
                            at = (2 * (t % 2) + e) * P
                            mm = pe.transpose(TBK[t // 2][:, at:at + P], VT2[:, e, tok(t)], idf[:, :])
                    mm.then_inc(v_turned, 1)

                def states(places, todo):
                    for bk, pair in places:
                        for q, i in enumerate(pair):
                            w, x = todo(i)
                            mm = pe.matmul(bank[bk][:, q * GLA_DV:(q + 1) * GLA_DV], w, x, start=True, stop=True)
                        mm.then_inc(ds_done, 1)

                def state_prompt():
                    def part(i):
                        rows = slice((i % 2) * GLA_CH, (i % 2 + 1) * GLA_CH)
                        return KEN[rows, i // 2, :], VN[rows, i // 2, :]
                    pe.wait_ge(v_copied, (h + 1).v)
                    states(DS_PROMPT, part)

                def state_sample():
                    pe.wait_ge(kem_ready, (h + 1).v)
                    pe.wait_ge(ds_read, (h * 8 + 4).v)
                    pe.wait_ge(at_ready, (h * 2 + 2).v)
                    states(DS_SAMPLE, lambda i: (KEM[:, i, :], VN[:, NTP, :]))

                def scores():
                    pe.wait_ge(q_ready, (h + 1).v)
                    for t in range(NT):
                        if t == 0:
                            pe.wait_ge(ds_read, (h * 8 + 4).v)
                        mm = pe.matmul(SBK[t // 4][:, (t % 4) * P:(t % 4 + 1) * P], KTl[:, tok(t)], QG[:, tok(t)],
                                       start=True, stop=True)
                        if t >= 3:
                            mm.then_inc(at_done, 1)

                def out(t):
                    O = (TBK[2], OBK)[t % 2]
                    if t == NTP:
                        pe.wait_ge(s0_in, (h * 16 + 16).v)
                    pe.wait_ge(at_ready, (h * 2 + (1 if t < NTP else 2)).v)
                    if t >= 2:
                        pe.wait_ge(go_read, (h * 5 + (t - 1)).v)
                    if t < NTP:
                        pe.matmul(O[:, 0:GLA_DV], AT[:, t, :], VN[:, t, :], start=True, stop=False)
                        for c in range(2):
                            mm = pe.matmul(O[c * GLA_CH:(c + 1) * GLA_CH, 0:GLA_DV], QG[:, t * P + c * GLA_CH:t * P + (c + 1) * GLA_CH],
                                           SA[:, 2 * t + c, :], start=False, stop=True)
                    else:
                        pe.matmul(O[:, 0:GLA_DV], AT[:, t, :], VN[:, t, :], start=True, stop=False)
                        for i in range(NB):
                            mm = pe.matmul(O[:, 0:GLA_DV], QGB[:, i, :], S0[:, i, :], start=False, stop=(i == NB - 1))
                    mm.then_inc(go_done, 1)

                def turn_o():
                    pe.wait_ge(go_ready, (h + 1).v)
                    pe.wait_ge(ds_read, (h * 8 + 8).v)
                    for t in range(NT):
                        for e in range(2):
                            mm = pe.transpose(TBK[t // 2][:, (2 * (t % 2) + e) * P:(2 * (t % 2) + e + 1) * P],
                                              OS[:, t, e * P:(e + 1) * P], idf[:, :])
                    mm.then_inc(gt_turned, 1)

                def both(*fs):
                    return lambda: [f() for f in fs]

                block(b, s, XH, XL, (gate, None))
                block(b + 1, 1 - s, XH, XL)
                block(b + 2, s, XH, XL, (turn_ke, None))
                block(b + 3, 1 - s, XH, XL, (turn_v, state_prompt))
                block(b + 4, s, XH, XL, (None, scores))
                block(b + 5, 1 - s, XH, XL, (both(*[lambda t=t: out(t) for t in (0, 1, 2, 3, 4)]),
                                            both(state_sample, turn_o)))

            gla_head(Lin(0))
            with pe.Fori(0, GLA_H - 1) as i:
                gla_head(Lin(1, (1, i)))
            merge(2, gy_done, 2 * GLA_H)

            def pairs(b0, n, AH, AL):
                with pe.Fori(0, n) as i:
                    for s in range(2):
                        block(b0.loop(2, i) + s, (b0.c + s) % 2, AH, AL)
            block(Lin(B_OUT), B_OUT % 2, YH, YL, a_ready=lambda h, k: pe.wait_ge(mix_split, k + 1) if h == 0 else None)
            block(Lin(B_OUT + 1), (B_OUT + 1) % 2, YH, YL)
            pairs(Lin(B_OUT + 2), KT // 2 - 1, YH, YL)

            def natural(n, t):
                c = n * NT + t
                if t >= 2:
                    pe.wait_ge(nat_free, c - 1)
                for k in range(KT):
                    mm = pe.transpose(bank[2 + 2 * (t % 2) + k // 4][:, (k % 4) * P:(k % 4 + 1) * P],
                                      (OTB, MIX)[n][:, k, tok(t)], idf[:, :])
                mm.then_inc(nat_pe, 1)

            for h in range(2):
                pe.wait_ge(z_free[h], B_MLP)
            natural(0, 0)
            for t in range(NT):
                if t + 1 < NT:
                    natural(0, t + 1)
                norm_turn(1, t, HS1)
            pe.wait_ge(nt_free, 4 * NT)

            def group(g, last=False):
                b = g * (2 * KT) + B_MLP
                pairs(b, KT // 2, XH, XL)

                def u_ready(h, k):
                    if h == 0 and k == 0:
                        pe.wait_ge(u_done[0], (g * KT + KT).v)
                        pe.wait_ge(u_done[1], (g * KT + KT).v)
                    if (h, k) in ((0, KT - 1), (1, 0)):
                        pe.wait_ge(u_done[h], (g * KT + (KT + 1)).v)
                block(b + KT, b.c % 2, YH, YL, a_ready=u_ready)
                block(b + (KT + 1), (b.c + 1) % 2, YH, YL)
                pairs(b + (KT + 2), KT // 2 - 1, YH, YL)

            with pe.Fori(0, NG - 1) as g:
                group(Lin(0, (1, g)))
            group(Lin(NG - 1))
            for h in range(2):
                pe.wait_ge(z_free[h], N_BLK)
            for t in range(NT):
                natural(1, t)

        @blk.gpsimd
        def _(pool):
            step = Steps(pool, pool_step)
            pool.memset(raw[0][:, :, :], 0.0).then_inc(pad_zero, 1)
            pool.memset(vrow[:, :], 0.0).then_inc(pad_zero, 1)
            step(pool.memset(idf[:, :], 0.0))
            pool.affine_select(out=idf[:, :], in_=idf[:, :], compare_op=ALU.not_equal, fill=1.0, base=0,
                               pattern=[[-1, P]], channel_multiplier=1).then_inc(consts, 1)
            pool.wait_ge(consts, 1)
            pool.tensor_copy(idb[:, :], idf[:, :]).then_inc(consts, 1)

            def blocks(m):
                return m[:, :].rearrange("p (b t) -> p b t", t=TS_)
            step(pool.memset(mask_p[:, :], 0.0))
            step(pool.affine_select(out=mask_p[:, :], in_=mask_p[:, :], compare_op=ALU.is_ge, fill=NEG, base=0,
                                    pattern=[[-1, P]], channel_multiplier=1))
            pool.affine_select(out=blocks(mask_s), in_=blocks(mask_p), compare_op=ALU.is_ge, fill=NEG, base=TS_ - 1,
                               pattern=[[TS_, NB], [0, TS_]], channel_multiplier=-1).then_inc(consts, 1)
            step(pool.memset(gmask_s[:, :], 1.0))
            step(pool.affine_select(out=gmask_s[:, :], in_=gmask_s[:, :], compare_op=ALU.is_ge, fill=0.0, base=0,
                                    pattern=[[1, P]], channel_multiplier=-1))
            pool.affine_select(out=gmask_p[:, :].rearrange("p (b t) -> p b t", t=GLA_CH),
                               in_=gmask_s[:, :].rearrange("p (b t) -> p b t", t=GLA_CH), compare_op=ALU.is_ge,
                               fill=0.0, base=0, pattern=[[-GLA_CH, P // GLA_CH], [0, GLA_CH]],
                               channel_multiplier=1).then_inc(consts, 1)
            pool.wait_ge(consts, 4)
            step(pool.affine_select(out=blocks(gmask_s), in_=blocks(gmask_s), compare_op=ALU.is_ge, fill=0.0, base=0,
                                    pattern=[[-TS_, NB], [0, TS_]], channel_multiplier=1))
            step(pool.memset(bmask[:, :], 1.0))
            step(pool.affine_select(out=bmask[:, :], in_=bmask[:, :], compare_op=ALU.is_ge, fill=0.0, base=0,
                                    pattern=[[-TS_, NB]], channel_multiplier=1))
            pool.affine_select(out=bmask[:, :], in_=bmask[:, :], compare_op=ALU.is_ge, fill=0.0, base=TS_ - 1,
                               pattern=[[TS_, NB]], channel_multiplier=-1).then_inc(consts, 1)

        SS, ROOT, RINV, LAM, LMIN, MX, NMX, RSUM, RSI = range(9)

        def one(v):
            while len(v.shape) > 2:
                v = v.rearrange("p a b -> p (a b)") if len(v.shape) == 3 else v.rearrange("p a b c -> p (a b) c")
            return v

        def at(n):
            return n.ds() if n.terms else slice(n.c, n.c + 1)

        @blk.scalar
        def _(act):
            step = Steps(act, act_step)

            def hi(b, s):
                act.wait_ge(raw_in[s], (b.half() * 16 + 16).v)
                if b.terms or b.c >= 2:
                    act.wait_ge(z_done[1], (b + -1).v)
                act.copy(WH[s][:, :, :], raw[s][:, :, :]).then_inc(w_hi, 1)

            def evac(b, h, dst, scale=1.0):
                act.wait_ge(z_done[h], (b + 1).v)
                act.activation(dst, Z[h][:, 0:HT], ACT.Copy, scale=scale).then_inc(z_free[h], 1)

            def norm_hi(n, t):
                for q in range(2):
                    c = 2 * (n * NT + t) + q
                    act.wait_ge(nt_done, c + 1)
                    act.copy(XH[:, 4 * q:4 * q + 4, tok(t)],
                             bank[(2 + 2 * (t % 2) if n == 0 else 6) + q].rearrange("p (k t) -> p k t", t=P)).then_inc(nt_hi, 1)

            def root(src, junk_, t, sig):
                step(act.activation(junk_, src, ACT.Square, accum_out=small[:, SS, t:t + 1]))
                act.activation(small[:, ROOT, t:t + 1], small[:, SS, t:t + 1], ACT.Sqrt, scale=1.0 / D,
                               bias=eps[:, :]).then_inc(sig, 1)

            act.wait_ge(eps_set, 1)
            for t in range(NT + 1):
                if t < NT:
                    act.wait_ge(x_in[t], 16)
                    root(XN[:, t, :], junk[:, :], t, root_done)
                if t >= 1:
                    norm_hi(0, t - 1)
            act.wait_ge(pad_in, 16)
            hi(Lin(0), 0)
            hi(Lin(1), 1)
            act.wait_ge(col_pe, 1)
            act.copy(col[:, :, :], bank[6][:, 0:KT * NR].rearrange("p (k r) -> p k r", r=NR)).then_inc(col_sb, 1)
            act.wait_ge(col_sb, 1)
            lam = small[:, LAM, :]
            step(act.activation(lam, col[:, :, R_LAM], ACT.Abs))
            step(act.activation(lam, lam, ACT.Exp, scale=-1.0))
            act.activation(lam, lam, ACT.Ln, bias=1.0).then_inc(lam_ln, 1)
            act.wait_ge(vec_in, 16 * 10)
            for h in range(2):
                act.wait_ge(z_done[h], 1)
                step(act.activation(fz[0:FOX_HEADS, h * HT:(h + 1) * HT], Z[h][0:FOX_HEADS, 0:HT], ACT.Identity, bias=bcol[:, :]))
                act.copy(glr[:, h * HT:(h + 1) * HT], Z[h][32:32 + GLA_RANK, 0:HT]).then_inc(z_free[h], 1)
            lf8, fz8 = lfT[0:FOX_HEADS, :], fz[0:FOX_HEADS, :]
            step(act.activation(lf8, fz8, ACT.Abs))
            step(act.activation(lf8, lf8, ACT.Exp, scale=-1.0))
            act.activation(lf8, lf8, ACT.Ln, bias=1.0).then_inc(ff_ln, 1)
            for part, dst in enumerate((QT, KTt, VTt)):
                b = B_FOX + part
                hi(Lin(b + 1), (b + 1) % 2)
                for h in range(2):
                    evac(Lin(b), h, dst[:, 0, h * HT:(h + 1) * HT], FOX_DH ** -0.5 if part == 0 else 1.0)

            def fox_window(a, par, proj):
                b = a * 3 + (B_FOX + 3)
                s = (B_FOX + 3 + par) % 2

                def take(part, h):
                    if proj:
                        evac(b + part, h, (QT, KTt, VTt)[part][:, 1 - par, h * HT:(h + 1) * HT],
                             FOX_DH ** -0.5 if part == 0 else 1.0)

                def exps(p):
                    t = ORD[p]
                    w = (t + 1) * P if t < NTP else PAST + P
                    act.wait_ge(m_ready, (a * 5 + (p + 1)).v)
                    act.activation(SP[:, p % 2, 0:w], SP[:, p % 2, 0:w], ACT.Exp, bias=small[:, NMX, p:p + 1],
                                   accum_out=small[:, RSUM, p:p + 1]).then_inc(p_ready, 1)

                def kv(j):
                    n = min(4, 2 * NT - 4 * j)
                    act.wait_ge(kv_turned, (a * 3 + (j + 1)).v)
                    if j == 0 and (a.terms or a.c > 0):
                        act.wait_ge(kv_stored, (a * 64).v)
                    act.copy(KVN[:, 4 * j:4 * j + n, :], TBK[j % 2][:, 0:n * P].rearrange("p (t d) -> p t d", d=P)).then_inc(kv_copied, 1)

                def y(p):
                    act.wait_ge(ot_turned, (a * 5 + (p + 1)).v)
                    act.copy(YH[:, at(a), tok(ORD[p])], OBK[:, P:2 * P].unsqueeze(1)).then_inc(y_hi, 1)

                if proj:
                    hi(b + 1, 1 - s)
                take(0, 0)
                exps(0)
                exps(1)
                take(0, 1)
                kv(0)
                if proj:
                    hi(b + 2, s)
                take(1, 0)
                exps(2)
                kv(1)
                kv(2)
                take(1, 1)
                y(0)
                exps(3)
                if proj:
                    hi(b + 3, 1 - s)
                take(2, 0)
                y(1)
                exps(4)
                take(2, 1)
                y(2)
                y(3)
                y(4)

            fox_window(Lin(0), 0, True)
            with step.loop(FOX_HEADS // 2 - 1, 0) as i:
                fox_window(Lin(1, (2, i)), 1, True)
                fox_window(Lin(2, (2, i)), 0, True)
            fox_window(Lin(FOX_HEADS - 1), 1, False)

            def merge(r):
                s = B_MG[r] % 2
                with step.loop(KT, 0) as j:
                    b = Lin(B_MG[r], (2, j))
                    hi(b + 1, 1 - s)
                    for h in range(2):
                        act.wait_ge(z_done[h], (b + 1).v)
                        act.activation(GT[:, h * HT:(h + 1) * HT], Z[h][:, 0:HT], ACT.Tanh, scale=0.5).then_inc(z_free[h], 1)
                    hi(b + 2, s)

            merge(0)

            def lru_window(n, cur, lag):
                b = n * 2 + B_LRU
                s = B_LRU % 2
                m = n + -1
                if cur:
                    hi(b + 1, 1 - s)
                if lag:
                    act.wait_ge(g_mm, n.v)
                    act.wait_ge(lru_cols, 1)
                    for dst, bk, r in ((RA, 2, R_BA), (RX, 4, R_BX)):
                        for h in range(2):
                            ins_ = act.activation(dst[:, h * HT:(h + 1) * HT], bank[bk + h][:, 0:HT], ACT.Tanh, scale=0.5,
                                                  bias=one(col[:, at(m), r:r + 1]))
                    ins_.then_inc(r_act, 1)
                    act.wait_ge(r_act, n.v)
                    c4, c4n = one(lru_c4[:, 0:1, at(m)]), one(lru_c4[:, 1:2, at(m)])
                    act.activation(TH[:, :], RA[:, :], ACT.Tanh, scale=c4n, bias=c4n)
                    step(act.activation(AA[:, :], RA[:, :], ACT.Exp, scale=c4, bias=c4))
                    act.activation(A2[:, :], AA[:, :], ACT.Square).then_inc(a_act, 1)
                if cur:
                    if n.terms or n.c > 0:
                        act.wait_ge(xc_ready, n.v)
                    act.wait_ge(z_done[0], (b + 1).v)
                    act.copy(XP[:, 3:3 + HT], Z[0][:, 0:HT]).then_inc(z_free[0], 1)
                if lag:
                    act.wait_ge(m_dve, n.v)
                    act.activation(MM[:, :], MM[:, :], ACT.Sqrt).then_inc(m_act, 1)
                if cur:
                    act.wait_ge(z_done[1], (b + 1).v)
                    act.copy(XP[:, 3 + HT:3 + TP], Z[1][:, 0:TP - HT])
                    act.copy(XPS[:, :, CONV_W - 1:], Z[1][:, TP - HT:HT].rearrange("p (b t) -> p b t", t=TS_)).then_inc(z_free[1], 1)
                if lag:
                    act.wait_ge(h_ready, n.v)
                    act.copy(YH[:, at(m), :], MM[:, :].unsqueeze(1)).then_inc(yl_hi, 1)
                if cur:
                    hi(b + 2, s)
                    if n.terms or n.c > 0:
                        act.wait_ge(ge_out, n.v)
                    for h in range(2):
                        evac(b + 1, h, LG[:, h * HT:(h + 1) * HT])
                    for h in range(2):
                        act.wait_ge(z_free[h], (b + 2).v)
                    act.activation(GQ[:, :], LG[:, :], ACT.Square).then_inc(ge_sq, 1)
                    act.wait_ge(ge_dve, (n + 1).v)
                    act.activation(TG[:, :], GQ[:, :], ACT.Tanh, scale=GELU_A).then_inc(ge_act, 1)

            act.wait_ge(y_done, 5 * FOX_HEADS)
            act.wait_ge(kv_stored, 64 * FOX_HEADS)
            lru_window(Lin(0), True, False)
            with step.loop(LRU_N - 1, 1) as i:
                lru_window(Lin(1, (1, i)), True, True)
            lru_window(Lin(LRU_N), False, True)
            merge(1)
            act.wait_ge(last_pe, 1)
            act.copy(LS[0:36, :], psum[0:36, 2:4, :].rearrange("p a b -> p (a b)")).then_inc(last_sb, 1)

            def gla_head(h):
                b = h * 6 + B_GLA
                s = B_GLA % 2
                some = bool(h.terms) or h.c > 0

                def half(v, q):
                    return v[:, q * HT:(q + 1) * HT]

                hi(b + 1, 1 - s)
                evac(b, 0, half(KG, 0))
                act.wait_ge(gg_mm, (h + 1).v)
                if some:
                    act.wait_ge(ds_read, (h * 8).v)
                for q in range(2):
                    ins_ = act.activation(half(ZG, q), SBK[q][:, 0:HT], ACT.Identity, bias=one(col[:, at(h), R_BG:R_BG + 1]))
                step(ins_)
                step(act.activation(E1[:, :], ZG[:, :], ACT.Abs))
                step(act.activation(E1[:, :], E1[:, :], ACT.Exp, scale=-1.0))
                act.activation(E2[:, :], E1[:, :], ACT.Ln, bias=1.0).then_inc(gg_act, 1)
                evac(b, 1, half(KG, 1))
                hi(b + 2, s)
                act.wait_ge(gg_dve, (h + 1).v)
                act.activation(E1[:, :], BC[:, :], ACT.Exp, scale=1.0 / GLA_TAU)
                act.activation(E2[:, :], BC[:, :], ACT.Exp, scale=-1.0 / GLA_TAU)
                act.activation(E3[:, :], E3[:, :], ACT.Exp, scale=1.0 / GLA_TAU).then_inc(ge3_act, 1)
                if some:
                    act.wait_ge(gy_done, (h * 2).v)
                for q in range(2):
                    evac(b + 1, q, half(VT2[:, 0, :], q))
                hi(b + 3, 1 - s)
                evac(b + 2, 0, half(VT2[:, 1, :], 0))
                act.wait_ge(ke_turned, (h + 1).v)
                act.wait_ge(ke_ready, (h + 1).v)
                act.copy(KEN[:, 0:4, :], TBK[0].rearrange("p (t d) -> p t d", d=P))
                act.copy(KEN[:, 4, :], TBK[1][:, 0:P]).then_inc(ken_ready, 1)
                evac(b + 2, 1, half(VT2[:, 1, :], 1))
                hi(b + 4, s)
                evac(b + 3, 0, half(QG, 0), GLA_DK ** -0.5)
                act.wait_ge(v_turned, (h + 1).v)
                for j in range(3):
                    n = 2 if j < 2 else 1
                    ins_ = act.copy(VN[:, 2 * j:2 * j + n, :], TBK[j][:, 0:n * GLA_DV].rearrange("p (t d) -> p t d", d=GLA_DV))
                ins_.then_inc(v_copied, 1)
                evac(b + 3, 1, half(QG, 1), GLA_DK ** -0.5)
                hi(b + 5, 1 - s)
                for e in range(2):
                    if e == 1:
                        hi(b + 6, s)
                    for q in range(2):
                        act.wait_ge(z_done[q], (b + (5 + e)).v)
                        act.activation(half(SG[:, e, :], q), Z[q][:, 0:HT], ACT.Tanh, scale=0.5).then_inc(sg_tanh, 1)
                        if (e, q) == (1, 0):
                            for t in range(NT):
                                O = (TBK[2], OBK)[t % 2]
                                act.wait_ge(go_done, (h * 5 + (t + 1)).v)
                                step(act.copy(OS[:, t, :], O[:, 0:GLA_DV]))
                                act.activation(E2[:, 0:GLA_DV], O[:, 0:GLA_DV], ACT.Square,
                                               accum_out=small[:, SS, t:t + 1]).then_inc(go_read, 1)
                            act.wait_ge(go_read, (h * 5 + 5).v)
                            act.activation(small[:, ROOT, 0:NT], small[:, SS, 0:NT], ACT.Sqrt, scale=1.0 / GLA_DV,
                                           bias=eps[:, :]).then_inc(go_root, 1)
                act.wait_ge(gt_turned, (h + 1).v)
                for j in range(3):
                    n = 2 if j < 2 else 1
                    for e in range(2):
                        src = TBK[j].rearrange("p (t e d) -> p t e d", e=2, d=P)[:, 0:n, e, :]
                        dst = OT[:, e, 2 * j * P:(2 * j + n) * P].rearrange("p (t d) -> p t d", d=P)
                        ins_ = act.activation(dst, src, ACT.Copy, scale=col[:, e, R_GN:R_GN + 1])
                    ins_.then_inc(gt_copied, 1)
                for e in range(2):
                    act.wait_ge(gy_dve, (h * 2 + (e + 1)).v)
                    act.copy(YH[:, h.ds(1, 2, e) if h.terms else slice(2 * h.c + e, 2 * h.c + e + 1), :],
                             OT[:, e, :].unsqueeze(1)).then_inc(gy_hi, 1)

            act.wait_ge(gla_init, 1)
            act.wait_ge(stored, 32 + 64)
            gla_head(Lin(0))
            with step.loop(GLA_H - 1, 8) as i:
                gla_head(Lin(1, (1, i)))
            act.wait_ge(gy_done, 2 * GLA_H)
            merge(2)

            for h in range(2):
                act.wait_ge(z_done[h], B_OUT)
            for k in range(KT):
                act.wait_ge(mix_sum, 2 * KT + k + 1)
                act.copy(YH[:, k, :], MIX[:, k, :]).then_inc(mix_hi, 1)

            def pairs(b0, n, per, body, n0=Lin(0)):
                with step.loop(n, per) as i:
                    for s in range(2):
                        b = b0.loop(2, i) + s
                        hi(b + 1, (b0.c + s + 1) % 2)
                        body(b, i * 2 + s, n0.loop(2, i) + s)

            def to_otb(b, j, _):
                for h in range(2):
                    evac(b, h, OTB[:, bass.ds(j, 1), h * HT:(h + 1) * HT].rearrange("p a b -> p (a b)"))
            pairs(Lin(B_OUT), KT // 2, 0, to_otb)

            for t in range(NT + 1):
                if t < NT:
                    act.wait_ge(nat_pe, t + 1)
                    root(psum[:, 2 + 2 * (t % 2):4 + 2 * (t % 2), :], NJ[:, :].rearrange("p (a b) -> p a b", b=512), t, nat_root)
                if t >= 1:
                    act.wait_ge(x2_ready, t)
                    root(X2[:, t - 1, :], NJ[:, :], t - 1, x2_root)
                    norm_hi(1, t - 1)

            def up(b, j, n):
                for h in range(2):
                    half = slice(h * HT, (h + 1) * HT)
                    act.wait_ge(z_done[h], (b + 1).v)
                    act.wait_ge(u_done[h], (n + 1).v)
                    act.activation(UR[:, half], Z[h][:, 0:HT], ACT.Relu).then_inc(z_free[h], 1)
                    act.wait_ge(z_free[h], (b + 1).v)
                    step(act.activation(UQ[:, half], UR[:, half], ACT.Square))
                    act.copy(YH[:, bass.ds(j, 1), half], UQ[:, half].unsqueeze(1)).then_inc(u_hi, 1)

            def group(g, last=False):
                b = g * (2 * KT) + B_MLP
                pairs(b, KT // 2, 4, up, g * KT)
                pairs(b + KT, KT // 2 - last, 0, lambda *_: None)
                if last:
                    hi(Lin(N_BLK - 1), (N_BLK - 1) % 2)

            with step.loop(NG - 1, 4 * KT // 2) as g:
                group(Lin(0, (1, g)))
            group(Lin(NG - 1), True)
            for t in range(NT):
                act.wait_ge(nat_pe, NT + t + 1)
                root(psum[:, 2 + 2 * (t % 2):4 + 2 * (t % 2), :], FJ[:, :].rearrange("p (a b) -> p a b", b=512), t, nat_root)

        @blk.vector
        def _(dve):
            step = Steps(dve, dve_step)

            def lo(b, s):
                dve.wait_ge(w_hi, (b + 1).v)
                dve.tensor_tensor(WL[s][:, :, :], raw[s][:, :, :], WH[s][:, :, :].bitcast(F32), ALU.subtract).then_inc(w_lo, 1)

            def norm_lo(n, t):
                for q in range(2):
                    c = 2 * (n * NT + t) + q
                    dve.wait_ge(nt_hi, c + 1)
                    dve.tensor_tensor(XL[:, 4 * q:4 * q + 4, tok(t)],
                                      bank[(2 + 2 * (t % 2) if n == 0 else 6) + q].rearrange("p (k t) -> p k t", t=P),
                                      XH[:, 4 * q:4 * q + 4, tok(t)].bitcast(F32), ALU.subtract).then_inc(nt_free, 1)

            def rinv(t, n=1):
                step(dve.reciprocal(small[:, RINV, t:t + n], small[:, ROOT, t:t + n]))

            def normed(n, t, x, g, HS):
                rinv(t)
                if t >= 2:
                    dve.wait_ge(nt_done, 2 * (n * NT + t - 2) + 2)
                dve.scalar_tensor_tensor(out=HS[:, t % 2, :], in0=x, scalar=small[:, RINV, t:t + 1], in1=g,
                                         op0=ALU.mult, op1=ALU.mult).then_inc(hs_done, 1)

            dve.memset(eps[:, :], EPS).then_inc(eps_set, 1)
            dve.memset(rst_p[0:FOX_HEADS, :], 1.0)
            step(dve.memset(rst_n[0:FOX_HEADS, :], 1.0))
            dve.memset(rst_p[0:FOX_HEADS, :].rearrange("p (b s) -> p b s", s=PAST)[:, :, 0:1], 0.0)
            step(dve.memset(by_sample(rst_n[0:FOX_HEADS, :])[:, :, 0:1], 0.0))
            dve.wait_ge(g_rows, 16)
            for t in range(NT + 1):
                if t < NT:
                    dve.wait_ge(root_done, t + 1)
                    normed(0, t, XN[:, t, :], G0[:, :], HS0)
                if t >= 1:
                    norm_lo(0, t - 1)
            lo(Lin(0), 0)
            lo(Lin(1), 1)
            dve.wait_ge(hs_done, NT)
            dve.memset(PM[:, :, :, :], 0.0)
            step(dve.memset(QB[:, :, :], 0.0))
            dve.wait_ge(col_sb, 1)
            step(dve.tensor_scalar(small[:, LMIN, :], col[:, :, R_LAM], 0.0, None, ALU.min))
            dve.tensor_scalar(col[:, :, R_BA:R_BX + 1], col[:, :, R_BA:R_BX + 1], 0.5, None, ALU.mult)
            dve.wait_ge(lam_ln, 1)
            step(dve.tensor_tensor(small[:, LMIN, :], small[:, LMIN, :], small[:, LAM, :], ALU.subtract))
            dve.tensor_scalar(lru_c4[:, 0, :], small[:, LMIN, :], 0.5 * LRU_C, None, ALU.mult)
            dve.tensor_scalar(lru_c4[:, 1, :], small[:, LMIN, :], -0.5 * LRU_C, None, ALU.mult).then_inc(lru_cols, 1)
            cp8, lf8, fz8, c8, nc8, rn8 = (v[0:FOX_HEADS, :] for v in (cpast, lfT, fz, cT, ncT, rst_n))
            for j in range(4):
                dve.wait_ge(cp_pe, j + 1)
                ins_ = dve.tensor_copy(cp8.rearrange("h (q r) -> h r q", r=16)[:, 4 * j:4 * j + 4, :],
                                       bank[2 + j][0:FOX_HEADS, :].rearrange("h (r q) -> h r q", q=P))
            step(ins_)
            step(dve.tensor_tensor_scan(cp8, rst_p[0:FOX_HEADS, :], cp8, 0.0, ALU.mult, ALU.add))
            dve.wait_ge(ff_ln, 1)
            dve.scalar_tensor_tensor(out=lf8, in0=fz8, scalar=0.0, in1=lf8, op0=ALU.min, op1=ALU.subtract).then_inc(ff_lf, 1)
            dve.wait_ge(ff_lf, 1)
            step(dve.tensor_copy(c8, lf8))
            step(dve.tensor_tensor(by_sample(c8)[:, :, 0:1], by_sample(c8)[:, :, 0:1],
                                   cp8.rearrange("h (b s) -> h b s", s=PAST)[:, :, PAST - 1:PAST], ALU.add))
            step(dve.tensor_tensor_scan(c8, rn8, c8, 0.0, ALU.mult, ALU.add))
            dve.tensor_scalar(nc8, c8, -1.0, None, ALU.mult).then_inc(ff_c, 1)
            dve.tensor_scalar(cp8, cp8, -1.0, None, ALU.mult).then_inc(cp_scan, 1)
            lo(Lin(2), 0)
            dve.wait_ge(lfn_pe, 1)
            dve.tensor_copy(lfn[:, :, :], bank[6][:, 0:NT * 8].rearrange("p (t h) -> p t h", h=8)).then_inc(lfn_sb, 1)
            lo(Lin(3), 1)
            dve.wait_ge(cn_pe, 1)
            dve.tensor_copy(cn[:, :, :], bank[7][:, 0:NT * 8].rearrange("p (t h) -> p t h", h=8)).then_inc(cn_sb, 1)
            dve.wait_ge(cn_sb, 1)
            lo(Lin(4), 0)

            def fox_window(a, par, proj):
                b = a * 3 + (B_FOX + 3)
                s = (B_FOX + 3 + par) % 2
                some = bool(a.terms) or a.c > 0

                def kc(j):
                    dve.wait_ge(kc_turned, (a * 4 + (j + 1)).v)
                    dve.tensor_copy(KCT[:, 4 * j:4 * j + 4, :], TBK[j % 2].rearrange("p (t d) -> p t d", d=P)).then_inc(kc_copied, 1)

                def soft(p):
                    t = ORD[p]
                    w, c0 = ((t + 1) * P, 0) if t < NTP else (PAST + P, TP)
                    if p < 2:
                        if some:
                            dve.wait_ge(p_turned, (a * 5).v)
                    else:
                        dve.wait_ge(p_turned, (a * 5 + (p - 1)).v)
                    dve.wait_ge(s_done, (a * 5 + (p + 1)).v)
                    dve.scalar_tensor_tensor(out=SP[:, p % 2, 0:w], in0=SBK[p % 2][:, 0:w], scalar=one(cn[:, t:t + 1, at(a)]),
                                             in1=CB[:, par, c0:c0 + w], op0=ALU.add, op1=ALU.add).then_inc(s_read, 1)
                    dve.wait_ge(s_read, (a * 5 + (p + 1)).v)
                    step(dve.tensor_reduce(small[:, MX, p:p + 1], SP[:, p % 2, 0:w], AX.X, ALU.max))
                    dve.tensor_scalar(small[:, NMX, p:p + 1], small[:, MX, p:p + 1], -1.0, None, ALU.mult).then_inc(m_ready, 1)

                def pt(p):
                    t = ORD[p]
                    dve.wait_ge(p_turned, (a * 5 + (p + 1)).v)
                    if p < 2:
                        if some:
                            dve.wait_ge(o_done, (a * 5).v)
                    else:
                        dve.wait_ge(o_done, (a * 5 + (p - 1)).v)
                    if t < NTP:
                        dve.tensor_copy(PTB[:, p % 2, 0:(t + 1) * P], TBK[2][:, 0:(t + 1) * P]).then_inc(p_copied, 1)
                    else:
                        for f in range(2):
                            dve.tensor_copy(diag(PM[:, f, :, :]), TBK[2][:, f * P:(f + 1) * P].rearrange("p (b t) -> p b t", t=TS_))
                        dve.tensor_copy(PTB[:, p % 2, 0:P], TBK[2][:, 2 * P:3 * P]).then_inc(p_copied, 1)

                def on(p):
                    step(dve.reciprocal(small[:, RSI, p:p + 1], small[:, RSUM, p:p + 1]))
                    dve.wait_ge(o_done, (a * 5 + (p + 1)).v)
                    dve.tensor_scalar(ON[:, p % 2, :], OBK[:, 0:P], small[:, RSI, p:p + 1], None, ALU.mult).then_inc(on_ready, 1)

                def y(p):
                    dve.wait_ge(y_hi, (a * 5 + (p + 1)).v)
                    dve.tensor_tensor(YL[:, at(a), tok(ORD[p])], OBK[:, P:2 * P].unsqueeze(1),
                                      YH[:, at(a), tok(ORD[p])].bitcast(F32), ALU.subtract).then_inc(y_done, 1)

                if proj:
                    lo(b + 1, 1 - s)
                dve.wait_ge(z_free[0], b.v)
                dve.wait_ge(z_free[1], b.v)
                if some:
                    dve.wait_ge(s_done, (a * 5).v)
                dve.tensor_copy(diag(QB), QT[:, par, TP:T].rearrange("p (b t) -> p b t", t=TS_)).then_inc(qb_ready, 1)
                kc(0)
                kc(1)
                dve.wait_ge(head_in[par], (a.half() * 80 + 80).v)
                soft(0)
                soft(1)
                kc(2)
                kc(3)
                pt(0)
                if proj:
                    lo(b + 2, s)
                soft(2)
                pt(1)
                on(0)
                y(0)
                soft(3)
                pt(2)
                on(1)
                if proj:
                    lo(b + 3, 1 - s)
                y(1)
                soft(4)
                pt(3)
                on(2)
                y(2)
                pt(4)
                on(3)
                y(3)
                on(4)
                y(4)

            fox_window(Lin(0), 0, True)
            with step.loop(FOX_HEADS // 2 - 1, 20) as i:
                fox_window(Lin(1, (2, i)), 1, True)
                fox_window(Lin(2, (2, i)), 0, True)
            fox_window(Lin(FOX_HEADS - 1), 1, False)

            def merge(r):
                s = B_MG[r] % 2
                with step.loop(KT, 1) as j:
                    b = Lin(B_MG[r], (2, j))
                    lo(b + 1, 1 - s)
                    lo(b + 2, s)
                    for h in range(2):
                        half = slice(h * HT, (h + 1) * HT)
                        m = MIX[:, bass.ds(j, 1), half].rearrange("p a b -> p (a b)")
                        dve.wait_ge(z_done[h], (b + 2).v)
                        dve.scalar_tensor_tensor(out=TMP[:, half], in0=GT[:, half], scalar=1.0, in1=Z[h][:, 0:HT],
                                                 op0=ALU.add, op1=ALU.mult).then_inc(z_free[h], 1)
                        dve.wait_ge(z_free[h], (b + 2).v)
                        if r == 0:
                            ins_ = dve.tensor_scalar(m, TMP[:, half], 0.5, None, ALU.mult)
                        else:
                            ins_ = dve.scalar_tensor_tensor(out=m, in0=TMP[:, half], scalar=0.5, in1=m, op0=ALU.mult, op1=ALU.add)
                        if h == 0:
                            step(ins_)
                        else:
                            ins_.then_inc(mix_sum, 1)

            merge(0)

            def lru_window(n, cur, lag):
                b = n * 2 + B_LRU
                s = B_LRU % 2
                m = n + -1
                if cur:
                    lo(b + 1, 1 - s)
                if lag:
                    dve.wait_ge(a_act, n.v)
                    dve.scalar_tensor_tensor(out=MM[:, :], in0=A2[:, :], scalar=1.0, in1=TH[:, :], op0=ALU.add,
                                             op1=ALU.mult).then_inc(m_dve, 1)
                    step(dve.scalar_tensor_tensor(out=UU[:, :], in0=RX[:, :], scalar=1.0, in1=XC[:, :], op0=ALU.add, op1=ALU.mult))
                    dve.wait_ge(m_act, n.v)
                    step(dve.scalar_tensor_tensor(out=UU[:, :], in0=UU[:, :], scalar=0.5, in1=MM[:, :], op0=ALU.mult, op1=ALU.mult))
                    h0 = col[:, at(m), R_H0:R_H0 + NB].rearrange("p a b -> p (a b)").unsqueeze(2)
                    first_a, first_u = by_sample(AA)[:, :, 0:1], by_sample(UU)[:, :, 0:1]
                    step(dve.tensor_tensor(fix[:, :, :], first_a, h0, ALU.mult))
                    step(dve.tensor_tensor(first_u, first_u, fix[:, :, :], ALU.add))
                    step(dve.memset(first_a, 0.0))
                    step(dve.tensor_tensor_scan(HH[:, :], AA[:, :], UU[:, :], 0.0, ALU.mult, ALU.add))
                    dve.scalar_tensor_tensor(out=MM[:, :], in0=Y2[:, :], scalar=0.5, in1=HH[:, :], op0=ALU.mult,
                                             op1=ALU.mult).then_inc(h_ready, 1)
                    dve.tensor_copy(last[:, at(m), 27:28], HH[:, TP - 1:TP].unsqueeze(1))
                    step(dve.tensor_copy(last[:, at(m), 28:36], by_sample(HH)[:, :, TS_ - 1:TS_].rearrange("p b o -> p o b")))
                    dve.wait_ge(yl_hi, n.v)
                    dve.tensor_tensor(YL[:, at(m), :], MM[:, :].unsqueeze(1), YH[:, at(m), :].bitcast(F32),
                                      ALU.subtract).then_inc(yl_done, 1)
                if cur:
                    for h in range(2):
                        dve.wait_ge(z_free[h], (b + 1).v)
                    step(dve.tensor_copy(XPS[:, :, 0:3], col[:, at(n), R_CONV0:R_CONV0 + 24].rearrange("p o (b j) -> p (o b) j", j=3)))
                    for j in range(CONV_W):
                        w = one(col[:, at(n), R_CW + j:R_CW + j + 1])
                        for src, dst in ((XP[:, j:j + TP], XC[:, 0:TP]), (XPS[:, :, j:j + TS_], by_sample(XC))):
                            if j == 0:
                                ins_ = dve.tensor_scalar(dst, src, w, one(col[:, at(n), R_CB:R_CB + 1]), ALU.mult, ALU.add)
                            else:
                                ins_ = dve.scalar_tensor_tensor(out=dst, in0=src, scalar=w, in1=dst, op0=ALU.mult, op1=ALU.add)
                        if j < CONV_W - 1:
                            step(ins_)
                    dve.tensor_copy(last[:, at(n), 0:3], XP[:, TP:TP + 3].unsqueeze(1))
                    dve.tensor_copy(last[:, at(n), 3:27].rearrange("p o (b j) -> p (o b) j", j=3), XPS[:, :, TS_:]).then_inc(xc_ready, 1)
                    lo(b + 2, s)
                    dve.wait_ge(ge_sq, (n + 1).v)
                    step(dve.tensor_scalar(GQ[:, :], GQ[:, :], GELU_B, 1.0, ALU.mult, ALU.add))
                    dve.tensor_tensor(GQ[:, :], GQ[:, :], LG[:, :], ALU.mult).then_inc(ge_dve, 1)
                    dve.wait_ge(ge_act, (n + 1).v)
                    dve.scalar_tensor_tensor(out=Y2[:, :], in0=TG[:, :], scalar=1.0, in1=LG[:, :], op0=ALU.add,
                                             op1=ALU.mult).then_inc(ge_out, 1)
                    dve.wait_ge(ge_out, (n + 1).v)

            step(dve.memset(XP[:, 0:CONV_W - 1], 0.0))
            lru_window(Lin(0), True, False)
            with step.loop(LRU_N - 1, 12) as i:
                lru_window(Lin(1, (1, i)), True, True)
            lru_window(Lin(LRU_N), False, True)
            dve.memset(fix[:, :, :], 0.0).then_inc(last_dve, 1)
            merge(1)

            def gla_head(h):
                b = h * 6 + B_GLA
                s = B_GLA % 2

                def half(v, q):
                    return v[:, q * HT:(q + 1) * HT]

                def silu(e, q):
                    dve.wait_ge(sg_tanh, (h * 4 + (2 * e + q + 1)).v)
                    v = half(SG[:, e, :], q)
                    dve.scalar_tensor_tensor(out=v, in0=v, scalar=1.0, in1=Z[q][:, 0:HT], op0=ALU.add,
                                             op1=ALU.mult).then_inc(z_free[q], 1)

                def add_state(i, places, dec, S, nxt, signal):
                    bk, q = next((bk, pair.index(i)) for bk, pair in places if i in pair)
                    ins_ = dve.scalar_tensor_tensor(out=S[:, nxt, :], in0=S[:, i, :], scalar=E1[:, dec:dec + 1],
                                                    in1=bank[bk][:, q * GLA_DV:(q + 1) * GLA_DV], op0=ALU.mult, op1=ALU.add)
                    if signal:
                        ins_.then_inc(ds_read, 1)
                    else:
                        step(ins_)

                lo(b + 1, 1 - s)
                dve.wait_ge(gg_act, (h + 1).v)
                step(dve.scalar_tensor_tensor(out=ZG[:, :], in0=ZG[:, :], scalar=0.0, in1=E2[:, :], op0=ALU.min, op1=ALU.subtract))
                step(dve.tensor_tensor_scan(BC[:, :], RG[:, :], ZG[:, :], 0.0, ALU.mult, ALU.add))
                for lo_, hi_, c in ((0, TP, GLA_CH), (TP, T, TS_)):
                    v, d = (w[:, lo_:hi_].rearrange("p (a b) -> p a b", b=c) for w in (BC, E3))
                    ins_ = dve.tensor_tensor(d, v[:, :, c - 1:c].broadcast_to((P, (hi_ - lo_) // c, c)), v, ALU.subtract)
                ins_.then_inc(gg_dve, 1)
                lo(b + 2, s)
                dve.wait_ge(ge3_act, (h + 1).v)
                for q in range(2):
                    dve.wait_ge(z_free[q], (b + 1).v)
                step(dve.tensor_tensor(KTl[:, :], KG[:, :], E2[:, :], ALU.mult))
                dve.tensor_tensor(KG[:, :], KG[:, :], E3[:, :], ALU.mult).then_inc(ke_ready, 1)
                lo(b + 3, 1 - s)
                dve.wait_ge(ken_ready, (h + 1).v)
                dve.tensor_tensor(KEM[:, :, :], KEN[:, NTP, :].unsqueeze(1).broadcast_to((P, NB, P)),
                                  bmask[:, :].unsqueeze(2).broadcast_to((P, NB, P)), ALU.mult).then_inc(kem_ready, 1)
                lo(b + 4, s)
                lo(b + 5, 1 - s)
                for q in range(2):
                    dve.wait_ge(z_free[q], (b + 4).v)
                step(dve.tensor_tensor(QG[:, :], QG[:, :], E1[:, :], ALU.mult))
                dve.tensor_copy(diag(QGB), by_sample(QG)).then_inc(q_ready, 1)
                for i in range(TP // GLA_CH):
                    if i % 4 == 0:
                        dve.wait_ge(ds_done, (h * 8 + (i // 2 + 2)).v)
                    if i > 0 and i % 2 == 0:
                        dve.wait_ge(ds_read, (h * 8 + (i // 2)).v)
                    add_state(i, DS_PROMPT, i * GLA_CH + GLA_CH - 1, SA, i + 1, i % 2 == 1)
                silu(0, 0)
                silu(0, 1)
                dve.wait_ge(at_done, (h * 2 + 1).v)
                dve.tensor_tensor(AT[:, 0:4, :], SBK[0].rearrange("p (t s) -> p t s", s=P),
                                  gmask_p[:, :].unsqueeze(1).broadcast_to((P, 4, P)), ALU.mult).then_inc(at_ready, 1)
                dve.wait_ge(at_done, (h * 2 + 2).v)
                dve.tensor_tensor(AT[:, 4, :], SBK[1][:, 0:P], gmask_s[:, :], ALU.mult).then_inc(at_ready, 1)
                lo(b + 6, s)
                silu(1, 0)
                dve.wait_ge(go_root, (h + 1).v)
                rinv(0, NT)
                for t in range(NT):
                    ins_ = dve.tensor_scalar(OS[:, t, :], OS[:, t, :], small[:, RINV, t:t + 1], None, ALU.mult)
                ins_.then_inc(go_ready, 1)
                silu(1, 1)
                dve.wait_ge(go_done, (h * 5 + 5).v)
                for i in range(NB):
                    if i % 2 == 0:
                        dve.wait_ge(ds_done, (h * 8 + (i // 2 + 5)).v)
                    add_state(i, DS_SAMPLE, TP + i * TS_ + TS_ - 1, S0, i, i % 2 == 1)
                dve.wait_ge(gt_copied, (h * 3 + 3).v)
                for e in range(2):
                    dve.scalar_tensor_tensor(out=OT[:, e, :], in0=SG[:, e, :], scalar=0.5, in1=OT[:, e, :], op0=ALU.mult,
                                             op1=ALU.mult).then_inc(gy_dve, 1)
                for e in range(2):
                    dve.wait_ge(gy_hi, (h * 2 + (e + 1)).v)
                    j = h.ds(1, 2, e) if h.terms else slice(2 * h.c + e, 2 * h.c + e + 1)
                    dve.tensor_tensor(YL[:, j, :], OT[:, e, :].unsqueeze(1), YH[:, j, :].bitcast(F32),
                                      ALU.subtract).then_inc(gy_done, 1)

            dve.wait_ge(stored, 32 + 64)
            dve.memset(QGB[:, :, :], 0.0)
            dve.memset(SA[:, 0, :], 0.0)
            step(dve.memset(RG[:, :], 1.0))
            dve.memset(RG[:, 0:TP].rearrange("p (a b) -> p a b", b=GLA_CH)[:, :, 0:1], 0.0)
            dve.memset(by_sample(RG)[:, :, 0:1], 0.0).then_inc(gla_init, 1)
            dve.wait_ge(gla_init, 1)
            gla_head(Lin(0))
            with step.loop(GLA_H - 1, 13) as i:
                gla_head(Lin(1, (1, i)))
            merge(2)

            for k in range(KT):
                dve.wait_ge(mix_hi, k + 1)
                dve.tensor_tensor(YL[:, k, :], MIX[:, k, :], YH[:, k, :].bitcast(F32), ALU.subtract).then_inc(mix_split, 1)

            def pairs(b0, n, per, body):
                with step.loop(n, per) as i:
                    for s in range(2):
                        b = b0.loop(2, i) + s
                        lo(b + 1, (b0.c + s + 1) % 2)
                        body(b, i * 2 + s)
            pairs(Lin(B_OUT), KT // 2, 0, lambda *_: None)

            def add_normed(n, t, g):
                dve.wait_ge(nat_root, n * NT + t + 1)
                rinv(t)
                src = psum[:, 2 + 2 * (t % 2):4 + 2 * (t % 2), :]
                tmp = (TM, FN)[n]
                dve.scalar_tensor_tensor(out=tmp.rearrange("p (a b) -> p a b", b=512), in0=src, scalar=small[:, RINV, t:t + 1],
                                         in1=g[:, :].rearrange("p (a b) -> p a b", b=512), op0=ALU.mult, op1=ALU.mult).then_inc(nat_free, 1)
                dve.wait_ge(nat_free, n * NT + t + 1)
                dve.tensor_tensor(X2[:, t, :], X2[:, t, :], tmp, ALU.add).then_inc((x2_ready, fin_ready)[n], 1)

            dve.wait_ge(x_again, 16 * 5)
            for t in range(NT + 1):
                if t < NT:
                    add_normed(0, t, G1)
                if t >= 1:
                    dve.wait_ge(x2_root, t)
                    normed(1, t - 1, X2[:, t - 1, :], G2[:, :], HS1)
                    norm_lo(1, t - 1)

            dve.wait_ge(hs_done, 2 * NT)
            dve.wait_ge(nt_done, 4 * NT)
            step(dve.memset(MIX[:, :, :], 0.0))
            for h in range(2):
                dve.memset(fix[:, h:h + 1, :], 0.0).then_inc(u_done[h], 1)

            def group(g, last=False):
                b = g * (2 * KT) + B_MLP
                up_hi = g * (2 * KT)

                with step.loop(KT // 2, 0) as i:
                    for s in range(2):
                        lo(b.loop(2, i) + (s + 1), (b.c + s + 1) % 2)
                        for h in range(2):
                            half = slice(h * HT, (h + 1) * HT)
                            dve.wait_ge(u_hi, (up_hi.loop(4, i) + (2 * s + h + 1)).v)
                            dve.tensor_tensor(YL[:, bass.ds(i * 2 + s, 1), half], UQ[:, half].unsqueeze(1),
                                              YH[:, bass.ds(i * 2 + s, 1), half].bitcast(F32), ALU.subtract).then_inc(u_done[h], 1)

                def down(b, j):
                    for h in range(2):
                        half = slice(h * HT, (h + 1) * HT)
                        m = MIX[:, j, half]
                        if len(m.shape) > 2:
                            m = m.rearrange("p a b -> p (a b)")
                        dve.wait_ge(z_done[h], (b + 1).v)
                        dve.tensor_tensor(m, m, Z[h][:, 0:HT], ALU.add).then_inc(z_free[h], 1)

                with step.loop(KT // 2 - last, 0) as i:
                    for s in range(2):
                        bb = (b + KT).loop(2, i) + s
                        lo(bb + 1, (b.c + s + 1) % 2)
                        down(bb, bass.ds(i * 2 + s, 1))
                if last:
                    lo(Lin(N_BLK - 1), (N_BLK - 1) % 2)
                    down(Lin(N_BLK - 2), KT - 2)
                    down(Lin(N_BLK - 1), KT - 1)

            with step.loop(NG - 1, 0) as g:
                group(Lin(0, (1, g)))
            group(Lin(NG - 1), True)
            for t in range(NT):
                add_normed(1, t, G3)


_INS = ['x_prompt', 'x_sample', 'cache_fox_k', 'cache_fox_v', 'cache_fox_logf', 'state_lru_conv', 'state_lru_h',
        'state_gla', 'norm_mix_pre', 'norm_mix_post', 'w_in', 'b_fox_f', 'lru_conv_w', 'lru_conv_b', 'lru_w_a',
        'lru_b_a', 'lru_w_x', 'lru_b_x', 'lru_lambda', 'gla_w_gate_up', 'gla_b_gate', 'gla_norm', 'w_branch',
        'w_out', 'norm_mlp_pre', 'norm_mlp_post', 'w_up', 'w_down']
_OUTS = [(1, 512, 1024), (8, 16, 1024), (1, 1, 512, 8, 128), (1, 1, 512, 8, 128), (1, 1, 512, 8), (1, 1, 3, 1024),
         (1, 1, 1024), (1, 1, 4, 128, 256), (1, 8, 16, 8, 128), (1, 8, 16, 8, 128), (1, 8, 16, 8), (1, 8, 3, 1024),
         (1, 8, 1024), (1, 8, 4, 128, 256)]


def kernel(**inputs):
    import numpy as _np
    import concourse.bacc as _bacc
    from concourse import mybir as _mybir
    from concourse.bass_utils import run_bass_kernel_spmd as _run

    nc = _bacc.Bacc("TRN2", target_bir_lowering=False, num_devices=1)
    arrays, ins, outs = {}, [], []
    for name in _INS:
        a = _np.ascontiguousarray(inputs[name])
        arrays[f"in_{name}_dram"] = a
        ins.append(nc.dram_tensor(f"in_{name}_dram", a.shape, _mybir.dt.from_np(a.dtype), kind="ExternalInput").ap())
    for i, shape in enumerate(_OUTS):
        outs.append(nc.dram_tensor(f"out_{i}_dram", shape, F32, kind="ExternalOutput").ap())
    build(nc, ins, outs)
    r = _run(nc, [arrays], core_ids=[0])
    return tuple(r.results[0][f"out_{i}_dram"] for i in range(len(_OUTS)))
```

```python
from contextlib import ExitStack, contextmanager

import concourse.bass as bass
from concourse import mybir

ALU = mybir.AluOpType
ACT = mybir.ActivationFunctionType
AX = mybir.AxisListType
F32 = mybir.dt.float32
F32R = mybir.dt.float32r
BF16 = mybir.dt.bfloat16

P = 128
NEG = -1.0e30
ARENA = 22600
EPS = 1e-6
FOX_HEADS, FOX_DH = 8, 128
LRU_N, CONV_W, LRU_C = 8, 4, 8.0
GLA_H, GLA_DK, GLA_DV, GLA_RANK, GLA_TAU, GLA_CH = 4, 128, 256, 16, 16.0, 64
GELU_A, GELU_B = 0.7978845608028654, 0.044715


class Lin:

    def __init__(self, c, *terms):
        self.c, self.terms = c, terms

    def __add__(self, k):
        return Lin(self.c + k, *self.terms)

    def __mul__(self, k):
        return Lin(self.c * k, *[(m * k, r) for m, r in self.terms])

    def half(self):
        return Lin(self.c // 2, *[(m // 2, r) for m, r in self.terms])

    def loop(self, per, reg):
        return Lin(self.c, *self.terms, (per, reg))

    @property
    def v(self):
        out = self.c
        for m, r in self.terms:
            out = r * m + out
        return out

    def ds(self, size=1, scale=1, off=0):
        return bass.ds((self * scale + off).v, size)


class Steps:

    def __init__(self, eng, sem):
        self.eng, self.sem, self.at = eng, sem, Lin(0)

    def __call__(self, ins):
        self.mark(ins)
        self.wait()

    def mark(self, ins):
        ins.then_inc(self.sem, 1)
        self.at = self.at + 1

    def wait(self, but=0):
        self.eng.wait_ge(self.sem, (self.at + -but).v)

    @contextmanager
    def loop(self, n, per):
        start = self.at
        with self.eng.Fori(0, n) as i:
            self.at = start.loop(per, i)
            yield i
            assert self.at.c - start.c == per, f"{self.sem.name}: {self.at.c - start.c} steps, not {per}"
        self.at = start + n * per


def build(nc, ins, outs):
    (x_prompt, x_sample, cache_k, cache_v, cache_lf, st_conv, st_h, st_gla, n_mix_pre, n_mix_post,
     w_in, b_fox, conv_w, conv_b, lru_wa, lru_ba, lru_wx, lru_bx, lru_lam, gla_up, gla_bg,
     gla_norm, w_branch, w_out, n_mlp_pre, n_mlp_post, w_up, w_down) = ins
    (y_p, y_s, fk_p, fv_p, flf_p, lc_p, lh_p, gs_p, fk_s, fv_s, flf_s, lc_s, lh_s, gs_s) = outs

    TP, D = x_prompt.shape[1], x_prompt.shape[2]
    NB, TS_ = x_sample.shape[0], x_sample.shape[1]
    T = TP + NB * TS_
    HT = T // 2
    NT = T // P
    NTP = TP // P
    KT = D // P
    PAST = cache_k.shape[2]
    FF = w_up.shape[2]
    NG = FF // D
    assert T == NT * P and NB * TS_ == P and PAST == 2 * P and D == 1024 and HT <= 512

    cff = 3 * D
    clx = cff + FOX_HEADS
    clg = clx + D
    cgq = clg + D
    cgk = cgq + GLA_H * GLA_DK
    cgv = cgk + GLA_H * GLA_DK
    clr = cgv + GLA_H * GLA_DV
    cgo = clr + GLA_RANK
    cmg = cgo + GLA_H * GLA_DV

    B_FOX = 1
    B_MG = [0, 0, 0]
    B_MG[0] = B_FOX + 3 * FOX_HEADS
    B_LRU = B_MG[0] + 2 * KT
    B_MG[1] = B_LRU + 2 * LRU_N
    B_GLA = B_MG[1] + 2 * KT
    B_MG[2] = B_GLA + 6 * GLA_H
    B_OUT = B_MG[2] + 2 * KT
    B_MLP = B_OUT + KT
    N_BLK = B_MLP + NG * 2 * KT

    R_CONV0, R_H0, R_CW, R_CB, R_BA, R_BX, R_LAM, R_BG, R_GN = 0, 24, 32, 36, 37, 38, 39, 40, 41
    NR = 42

    w_in_v = w_in[0].rearrange("(k p) n -> p k n", p=P)
    w_br_v = [w_branch[0, r].rearrange("(k p) n -> p k n", p=P) for r in range(3)]
    w_out_v = w_out[0].rearrange("(k p) n -> p k n", p=P)
    w_up_v = w_up[0].rearrange("(k p) n -> p k n", p=P)
    w_dn_v = w_down[0].rearrange("(g k p) n -> g p k n", p=P, k=KT)

    with ExitStack() as ctx:
        def sb(name, shape, dt=F32):
            return ctx.enter_context(nc.sbuf_tensor(name, shape, dt))

        def sem(name):
            return ctx.enter_context(nc.semaphore(name))

        psum = ctx.enter_context(nc.psum_tensor("psum", [P, 8, 512], F32))
        bank = [psum[:, i, :] for i in range(8)]
        Z = bank[0:2]
        SBK = bank[2:4]
        TBK = bank[4:7]
        OBK = bank[7]
        OB = [OBK] * 4 + [SBK[1]]

        XH = sb("XH", [P, KT, T], F32R)
        XL = sb("XL", [P, KT, T], F32R)
        YH = sb("YH", [P, KT, T], F32R)
        YL = sb("YL", [P, KT, T], F32R)
        raw = [sb(f"w_raw{s}", [P, KT, P]) for s in range(2)]
        WH = [sb(f"w_hi{s}", [P, KT, P], F32R) for s in range(2)]
        WL = [sb(f"w_lo{s}", [P, KT, P], F32R) for s in range(2)]
        idf = sb("ident", [P, P])
        idb = sb("ident_bf", [P, P], BF16)
        mask_p = sb("mask_prompt", [P, P], BF16)
        mask_s = sb("mask_sample", [P, P], BF16)
        gmask_p = sb("gmask_prompt", [P, P])
        gmask_s = sb("gmask_sample", [P, P])
        bmask = sb("bmask", [P, NB])
        col = sb("col", [P, KT, NR])
        lru_c4 = sb("lru_c4", [P, 2, LRU_N])
        bcol = sb("b_fox_col", [FOX_HEADS, 1])
        glr = sb("glr", [GLA_RANK, T])
        cn = sb("c_nat", [P, NT, FOX_HEADS])
        small = sb("small", [P, 12, 8])
        eps = sb("eps", [P, 1])
        fix = sb("fix", [P, NB, 1])
        last = sb("last", [P, LRU_N, 36])
        GT = sb("gates", [P, 2, T])
        arena = sb("arena", [P, ARENA])

        def carve(start, *shapes):
            out, at = [], start
            for shape in shapes:
                n = 1
                for s in shape:
                    n *= s
                v = arena[:, at:at + n]
                if len(shape) == 2:
                    v = v.rearrange("p (a b) -> p a b", b=shape[1])
                if len(shape) == 3:
                    v = v.rearrange("p (a b c) -> p a b c", b=shape[1], c=shape[2])
                out.append(v)
                at += n
            assert at <= ARENA, at
            return out if len(out) > 1 else out[0]

        MIX = carve(0, (KT, T))
        A0 = KT * T

        nc_new = nc.dram_tensor("negc_new", (FOX_HEADS, T), F32, kind="Internal").ap()
        nc_past = nc.dram_tensor("negc_past", (FOX_HEADS, NB, PAST), F32, kind="Internal").ap()

        def sems(names):
            return [sem(n) for n in names.split()]

        raw_in = sems("raw_in0 raw_in1")
        w_hi, w_lo = sems("w_hi w_lo")
        z_done = sems("z_done0 z_done1")
        z_free = sems("z_free0 z_free1")
        dve_step, act_step, pool_step = sems("dve_step act_step pool_step")
        consts, pad_zero, pad_in, vec_in, lfc_in, g_rows, scr_out, stored = sems(
            "consts pad_zero pad_in vec_in lfc_in g_rows scr_out stored")
        eps_set, gla_init = sems("eps_set gla_init")
        x_in = [sem(f"x_in{t}") for t in range(NT)]
        root_done, hs_done, nt_done, nt_hi, nt_free = sems("root_done hs_done nt_done nt_hi nt_free")
        col_pe, col_sb, lam_ln, lru_cols = sems("col_pe col_sb lam_ln lru_cols")
        ff_ln, ff_lf, ff_c, cp_pe, cp_scan, cn_pe, lfn_pe, lfn_sb, cn_sb = sems(
            "ff_ln ff_lf ff_c cp_pe cp_scan cn_pe lfn_pe lfn_sb cn_sb")
        head_in = sems("head_in0 head_in1")
        kc_turned, kc_copied, kv_turned, kv_copied, kv_stored = sems(
            "kc_turned kc_copied kv_turned kv_copied kv_stored")
        qb_ready, s_done, s_read, m_ready, p_ready, p_normed, p_turned, p_copied = sems(
            "qb_ready s_done s_read m_ready p_ready p_normed p_turned p_copied")
        o_done, y_hi, y_done = sems("o_done y_hi y_done")
        mix_sum = sem("mix_sum")
        wg_in, xc_ready, g_mm, rx_act, r_act, a_act, m_dve, m_act, h_ready, yl_hi, yl_done = sems(
            "wg_in xc_ready g_mm rx_act r_act a_act m_dve m_act h_ready yl_hi yl_done")
        ge_sq, ge_dve, ge_act, ge_out, last_dve, last_pe, last_sb = sems(
            "ge_sq ge_dve ge_act ge_out last_dve last_pe last_sb")
        gu_in, s0_in, gs_stored, gg_mm, gg_act, gg_dve, ge3_act = sems(
            "gu_in s0_in gs_stored gg_mm gg_act gg_dve ge3_act")
        ke_ready, ke_turned, ken_ready, kem_ready, v_turned, v_copied, ds_done, ds_read = sems(
            "ke_ready ke_turned ken_ready kem_ready v_turned v_copied ds_done ds_read")
        q_ready, at_done, at_ready, go_done, go_read, go_root, go_ready = sems(
            "q_ready at_done at_ready go_done go_read go_root go_ready")
        sg_tanh, gt_turned, gt_copied, gy_dve, gy_hi, gy_done = sems(
            "sg_tanh gt_turned gt_copied gy_dve gy_hi gy_done")
        mix_hi, mix_split, nat_pe, nat_free, x_again, nat_root, x2_ready, x2_last, x2_root = sems(
            "mix_hi mix_split nat_pe nat_free x_again nat_root x2_ready x2_last x2_root")
        mlp_zero, u_hi = sems("mlp_zero u_hi")
        u_done = sems("u_done0 u_done1")
        fin_pool, fin_dve = sems("fin_pool fin_dve")

        XN = carve(0, (NT, D))
        HS0, vrow, junk, G0 = carve(A0, (2, D), (D,), (D,), (D,))
        cp_raw, cpast, rst_p, lfT, cT, ncT, rst_n, fz, lfn = carve(
            A0 + 10240 - 1024, (P,), (NB * PAST,), (NB * PAST,), (T,), (T,), (T,), (T,), (T,), (NT, FOX_HEADS))
        QT, KTt, VTt, KVN, KC0, KC1, VC0, VC1, CB, SP, PTB = carve(
            A0, (2, T), (2, T), (2, T), (2 * NT, P), (2 * NB, P), (2 * NB, P), (2 * NB, P), (2 * NB, P),
            (2, 896), (2, 512), (2, 512))
        KC, VC = (KC0, KC1), (VC0, VC1)
        KCT, PM, QB = carve(0, (2 * NB, P), (2, NB, P), (NB, P))
        XPW = CONV_W - 1 + TP + NB * (CONV_W - 1 + TS_)
        (WG, LG, GQ, TG, Y2, RA, RX, AA, TH, A2, MM, UU, HH, XC, XP, LS) = carve(
            A0, (2, P), (T,), (T,), (T,), (T,), (T,), (T,), (T,), (T,), (T,), (T,), (T,), (T,), (T,), (XPW + 1,), (D,))
        XPS = XP[:, CONV_W - 1 + TP:XPW].rearrange("p (b t) -> p b t", b=NB)
        (QG, KG, KTl, ZG, BC, E1, E2, E3, KEM, VT2, VN, QGB, S0, SA, OS, RG, GU, SG) = carve(
            A0, (T,), (T,), (T,), (T,), (T,), (T,), (T,), (T,), (NB, P), (2, T), (NT, GLA_DV),
            (NB, P), (NB, GLA_DV), (TP // GLA_CH + 1, GLA_DV), (NT, GLA_DV), (T,), (P,), (2, T))
        AT = ZG.rearrange("p (a b) -> p a b", b=P)
        KEN = BC.rearrange("p (a b) -> p a b", b=P)
        OT = VT2
        OTB, X2, G1, G2, G3 = carve(A0, (KT, T), (NT, D), (D,), (D,), (D,))
        HS1, NJ, TM = carve(0, (2, D), (D,), (2, D))
        UR, UQ = carve(A0, (T,), (T,))
        FN, FJ = carve(A0, (2, D), (D,))

        blk = ctx.enter_context(nc.Block())

        def halves(v):
            return v[:, 0:HT], v[:, HT:T]

        def by_sample(v):
            return v[:, TP:T].rearrange("p (b t) -> p b t", t=TS_)

        def diag(v):
            return bass.AP(tensor=v.tensor, offset=v.offset, ap=[v.ap[0], [P + TS_, NB], [1, TS_]])

        def tok(t):
            return slice(t * P, (t + 1) * P)

        DS_PROMPT = ((2, (0, 2)), (4, (1, 3)), (3, (4, 6)), (5, (5, 7)))
        DS_SAMPLE = ((2, (0, 1)), (3, (2, 3)), (4, (4, 5)), (5, (6, 7)))
        FIN_COUNT = (1, 1, 2, 2, 3)
        ORD = (0, 1, 4, 2, 3)

        @blk.sync
        def _(sp):
            def load(b, s, src):
                if not (isinstance(b, Lin) and not b.terms and b.c < 2):
                    sp.wait_ge(w_lo, (b + -1).v)
                sp.dma_start(raw[s][:, :, :], src).then_inc(raw_in[s], 16)

            for t in range(NTP):
                sp.dma_start(XN[:, t, :], x_prompt[0, t * P:(t + 1) * P, :]).then_inc(x_in[t], 16)
                if t == 0:
                    sp.dma_start(G0[:, :], n_mix_pre[0:1, :].broadcast_to((P, D))).then_inc(g_rows, 16)
            sp.dma_start(XN[:, NTP, :], x_sample.rearrange("b t d -> (b t) d")).then_inc(x_in[NTP], 16)
            sp.wait_ge(pad_zero, 2)
            sp.dma_start(raw[0][:, :, 0:FOX_HEADS], w_in_v[:, :, cff:cff + FOX_HEADS]).then_inc(raw_in[0], 16)
            sp.dma_start(raw[0][:, :, 32:32 + GLA_RANK], w_in_v[:, :, clr:clr + GLA_RANK]).then_inc(pad_in, 16)
            for r, v in ((R_CONV0, st_conv[0].rearrange("b j c -> (b j) c")), (R_H0, st_h[0]), (R_CW, conv_w[0]),
                         (R_CB, conv_b), (R_BA, lru_ba), (R_BX, lru_bx), (R_LAM, lru_lam)):
                sp.dma_start(vrow[r:r + v.shape[0], :], v).then_inc(vec_in, 16)
            sp.dma_start(vrow[R_BG:R_BG + 1, 0:GLA_H * GLA_DK], gla_bg).then_inc(vec_in, 16)
            sp.dma_start(vrow[R_GN:R_GN + 1, 0:GLA_DV], gla_norm).then_inc(vec_in, 16)
            sp.dma_start(bcol[:, :], b_fox.rearrange("o h -> h o")).then_inc(vec_in, 16)
            sp.dma_start(cp_raw[:, :], cache_lf[0].rearrange("b (q r) h -> (b q) (r h)", r=16)).then_inc(lfc_in, 16)

            def w_fox(h, part):
                return w_in_v[:, :, h.ds(P, P, part * D)] if h.terms else w_in_v[:, :, part * D + h.c * P:part * D + (h.c + 1) * P]

            def load_cache(c, dst, hd, par):
                sp.dma_start(dst[:, :, :], c[0].rearrange("b (f p) h d -> p (b f) h d", p=P)[:, :, hd, :]
                             .rearrange("p f o d -> p f (o d)")).then_inc(head_in[par], 16)

            def load_heads(h, par):
                hd = h.ds() if h.terms else slice(h.c, h.c + 1)
                if h.terms or h.c > 0:
                    load_cache(cache_k, KC[par], hd, par)
                load_cache(cache_v, VC[par], hd, par)
                sp.dma_start(CB[:, par, 0:TP], nc_new[hd, 0:TP].broadcast_to((P, TP))).then_inc(head_in[par], 16)
                sp.dma_start(CB[:, par, TP:TP + PAST], nc_past[hd, :, :].rearrange("o b s -> (o b) s")
                             .unsqueeze(1).broadcast_to((NB, TS_, PAST))).then_inc(head_in[par], 16)
                sp.dma_start(CB[:, par, TP + PAST:], nc_new[hd, TP:T].broadcast_to((P, P))).then_inc(head_in[par], 16)

            def store_kv(a):
                hd = a.ds() if a.terms else slice(a.c, a.c + 1)
                sp.wait_ge(kv_copied, (a * 3 + 3).v)
                for dp, ds_, at in ((fv_p, fv_s, 0), (fk_p, fk_s, NT)):
                    sp.dma_start(dp[0, 0, :, hd, :].rearrange("(t p) o d -> p t (o d)", p=P),
                                 KVN[:, at:at + NTP, :]).then_inc(kv_stored, 16)
                    sp.dma_start(ds_[0, :, :, hd, :].rearrange("b t o d -> (b t) (o d)"),
                                 KVN[:, at + NTP, :]).then_inc(kv_stored, 16)

            def fox_window(a, par, proj):
                b = a * 3 + (B_FOX + 3)
                s = (B_FOX + 3 + par) % 2
                if proj:
                    if a.terms or a.c > 0:
                        load(b, s, w_fox(a + 1, 0))
                    load(b + 1, 1 - s, w_fox(a + 1, 1))
                    if a.terms or a.c > 0:
                        sp.wait_ge(o_done, (a * 5).v)
                    load_heads(a + 1, 1 - par)
                    load(b + 2, s, w_fox(a + 1, 2))
                store_kv(a)

            for part in range(2):
                load(Lin(B_FOX + part), (B_FOX + part) % 2, w_fox(Lin(0), part))
            load_cache(cache_k, KC[0], slice(0, 1), 0)
            sp.wait_ge(ff_c, 1)
            sp.dma_start(nc_new, ncT[0:FOX_HEADS, :]).then_inc(scr_out, 16)
            sp.wait_ge(cp_scan, 1)
            sp.dma_start(nc_past, cpast[0:FOX_HEADS, :].rearrange("h (b s) -> h b s", s=PAST)).then_inc(scr_out, 16)
            load(Lin(B_FOX + 2), (B_FOX + 2) % 2, w_fox(Lin(0), 2))
            sp.wait_ge(lfn_sb, 1)
            sp.dma_start(flf_p[0, 0].rearrange("(t p) h -> p t h", p=P), lfn[:, 0:NTP, :]).then_inc(stored, 16)
            sp.dma_start(flf_s[0].rearrange("b t h -> (b t) h"), lfn[:, NTP, :]).then_inc(stored, 16)
            load(Lin(B_FOX + 3), (B_FOX + 3) % 2, w_fox(Lin(1), 0))
            sp.wait_ge(scr_out, 32)
            sp.wait_ge(cn_sb, 1)
            sp.wait_ge(stored, 32)
            load_heads(Lin(0), 0)
            fox_window(Lin(0), 0, True)
            with sp.Fori(0, FOX_HEADS // 2 - 1) as i:
                fox_window(Lin(1, (2, i)), 1, True)
                fox_window(Lin(2, (2, i)), 0, True)

            def gate_load(r, j, b):
                c0 = cmg + r * D
                load(b, b.c % 2, w_in_v[:, :, j.ds(P, P, c0) if j.terms else slice(c0 + j.c * P, c0 + (j.c + 1) * P)])

            def branch_load(r, j, b):
                load(b, b.c % 2, w_br_v[r][:, :, j.ds(P, P) if j.terms else slice(j.c * P, (j.c + 1) * P)])

            def merge_begin(r):
                gate_load(r, Lin(0), Lin(B_MG[r]))
                gate_load(r, Lin(1), Lin(B_MG[r] + 1))
                branch_load(r, Lin(0), Lin(B_MG[r] + 2))

            def merge(r):
                with sp.Fori(0, KT - 2) as i:
                    gate_load(r, Lin(2, (1, i)), Lin(B_MG[r] + 3, (2, i)))
                    branch_load(r, Lin(1, (1, i)), Lin(B_MG[r] + 4, (2, i)))
                branch_load(r, Lin(KT - 1), Lin(B_MG[r] + 2 * KT - 1))

            merge_begin(0)
            fox_window(Lin(FOX_HEADS - 1), 1, False)
            merge(0)

            def lru_loads(n, first=False):
                b = n * 2 + B_LRU
                c = (lambda c0: n.ds(P, P, c0) if n.terms else slice(c0 + n.c * P, c0 + (n.c + 1) * P))
                load(b, B_LRU % 2, w_in_v[:, :, c(clx)])
                load(b + 1, 1 - B_LRU % 2, w_in_v[:, :, c(clg)])
                if not first:
                    sp.wait_ge(g_mm, n.v)
                nd = n.ds() if n.terms else slice(n.c, n.c + 1)
                for i, w in enumerate((lru_wa, lru_wx)):
                    sp.dma_start(WG[:, i, :], w[0, nd].rearrange("n i j -> (n i) j")).then_inc(wg_in, 16)

            sp.wait_ge(y_done, 5 * FOX_HEADS)
            sp.wait_ge(kv_stored, 64 * FOX_HEADS)
            lru_loads(Lin(0), True)
            with sp.Fori(0, LRU_N - 1) as i:
                lru_loads(Lin(1, (1, i)))
            merge_begin(1)
            merge(1)
            sp.wait_ge(last_sb, 1)
            sp.dma_start(lc_p[0, 0], LS[0:3, :]).then_inc(stored, 16)
            sp.dma_start(lc_s[0].rearrange("b j c -> (b j) c"), LS[3:27, :]).then_inc(stored, 16)
            sp.dma_start(lh_p[0], LS[27:28, :]).then_inc(stored, 16)
            sp.dma_start(lh_s[0], LS[28:36, :]).then_inc(stored, 16)
            load(Lin(B_GLA), B_GLA % 2, w_in_v[:, :, cgk:cgk + P])
            sp.wait_ge(stored, 32 + 64)

            def gla_loads(h, first=False):
                b = h * 6 + B_GLA
                s = B_GLA % 2
                hd = h.ds() if h.terms else slice(h.c, h.c + 1)

                def c(c0, per, off=0):
                    return h.ds(P, per, c0 + off) if h.terms else slice(c0 + off + h.c * per, c0 + off + h.c * per + P)
                if not first:
                    load(b, s, w_in_v[:, :, c(cgk, P)])
                    sp.wait_ge(gg_mm, h.v)
                sp.dma_start(GU[0:GLA_RANK, :], gla_up[0][:, c(0, P)]).then_inc(gu_in, 16)
                load(b + 1, 1 - s, w_in_v[:, :, c(cgv, GLA_DV)])
                load(b + 2, s, w_in_v[:, :, c(cgv, GLA_DV, P)])
                if not first:
                    store_states(h + -1)
                    sp.wait_ge(gs_stored, (h * 32).v)
                sp.dma_start(S0[:, :, :], st_gla[0][:, hd].rearrange("b o k v -> k b (o v)")).then_inc(s0_in, 16)
                load(b + 3, 1 - s, w_in_v[:, :, c(cgq, P)])
                load(b + 4, s, w_in_v[:, :, c(cgo, GLA_DV)])
                load(b + 5, 1 - s, w_in_v[:, :, c(cgo, GLA_DV, P)])

            def store_states(h):
                hd = h.ds() if h.terms else slice(h.c, h.c + 1)
                sp.wait_ge(ds_read, (h * 8 + 8).v)
                sp.dma_start(gs_p[0, 0][hd].rearrange("o k v -> (o k) v"), SA[:, TP // GLA_CH, :]).then_inc(gs_stored, 16)
                sp.dma_start(gs_s[0][:, hd].rearrange("b o k v -> k b (o v)"), S0[:, :, :]).then_inc(gs_stored, 16)

            gla_loads(Lin(0), True)
            with sp.Fori(0, GLA_H - 1) as i:
                gla_loads(Lin(1, (1, i)))
            merge_begin(2)
            store_states(Lin(GLA_H - 1))
            merge(2)
            sp.wait_ge(gy_done, 2 * GLA_H)
            sp.wait_ge(gs_stored, 32 * GLA_H)
            for g, v in ((G1, n_mix_post), (G2, n_mlp_pre), (G3, n_mlp_post)):
                sp.dma_start(g[:, :], v[0:1, :].broadcast_to((P, D))).then_inc(x_again, 16)
            sp.dma_start(X2[:, 0:NTP, :], x_prompt[0].rearrange("(t p) d -> p t d", p=P)).then_inc(x_again, 16)
            sp.dma_start(X2[:, NTP, :], x_sample.rearrange("b t d -> (b t) d")).then_inc(x_again, 16)
            with sp.Fori(0, KT // 2) as i:
                for s in range(2):
                    load(Lin(B_OUT + s, (2, i)), (B_OUT + s) % 2, w_out_v[:, :, bass.ds(i * (2 * P) + s * P, P)])

            def up_loads(b, g, n):
                with sp.Fori(0, n) as j:
                    for s in range(2):
                        cols = j * (2 * P) + ((g * D + s * P) if isinstance(g, int) else g * D + s * P)
                        load(b.loop(2, j) + s, (B_MLP + s) % 2, w_up_v[:, :, bass.ds(cols, P)])

            def down_loads(b, g, n):
                with sp.Fori(0, n) as j:
                    for s in range(2):
                        w = w_dn_v[g] if isinstance(g, int) else w_dn_v[bass.ds(g, 1)].rearrange("o p k n -> (o p) k n")
                        load(b.loop(2, j) + s, (B_MLP + s) % 2, w[:, :, bass.ds(j * (2 * P) + s * P, P)])


            up_loads(Lin(B_MLP), 0, KT // 2)
            down_loads(Lin(B_MLP + KT), 0, KT // 2)
            with sp.Fori(1, NG) as g:
                up_loads(Lin(B_MLP, (2 * KT, g)), g, KT // 2)
                down_loads(Lin(B_MLP + KT, (2 * KT, g)), g, KT // 2)
            for t in range(NT):
                sp.wait_ge((fin_pool, fin_dve)[t % 2 or t == NT - 1], FIN_COUNT[t])
                dst = y_p[0, t * P:(t + 1) * P, :] if t < NTP else y_s.rearrange("b t d -> (b t) d")
                sp.dma_start(dst, X2[:, t, :]).then_inc(stored, 16)
            sp.wait_ge(stored, 32 + 64 + 16 * NT)
            sp.wait_ge(kv_stored, 64 * FOX_HEADS)
            sp.wait_ge(gs_stored, 32 * GLA_H)
            sp.wait_ge(scr_out, 32)

        @blk.tensor
        def _(pe):
            def block(b, s, AH, AL, after=(None, None), a_ready=None):
                pe.wait_ge(w_lo, (b + 1).v)
                for h in range(2):
                    if b.terms or b.c > 0:
                        pe.wait_ge(z_free[h], b.v)
                    for k in range(KT):
                        if a_ready is not None:
                            a_ready(h, k)
                        for i, (w, x) in enumerate(((WH, AH), (WH, AL), (WL, AH))):
                            mm = pe.matmul(Z[h][:, 0:HT], w[s][:, k, :], x[:, k, h * HT:(h + 1) * HT],
                                           start=(k == 0 and i == 0), stop=(k == KT - 1 and i == 2))
                    mm.then_inc(z_done[h], 1)
                    if after[h] is not None:
                        after[h]()

            def norm_turn(n, t, HS):
                c = n * NT + t
                pe.wait_ge(hs_done, c + 1)
                for q in range(2):
                    bk = bank[(2 + 2 * (t % 2) if n == 0 else 6) + q]
                    back = 2 - n
                    if t >= back:
                        pe.wait_ge(nt_free, 2 * (c - back) + q + 1)
                    for k in range(4):
                        mm = pe.transpose(bk[:, k * P:(k + 1) * P], HS[:, t % 2, (4 * q + k) * P:(4 * q + k + 1) * P], idf[:, :])
                    mm.then_inc(nt_done, 1)

            pe.wait_ge(consts, 2)
            for t in range(NT):
                norm_turn(0, t, HS0)
            pe.wait_ge(vec_in, 16 * 10)
            for k in range(KT):
                mm = pe.transpose(bank[6][:, k * NR:(k + 1) * NR], vrow[0:NR, k * P:(k + 1) * P], idf[0:NR, 0:NR])
            mm.then_inc(col_pe, 1)
            pe.wait_ge(nt_free, 2 * NT)
            block(Lin(0), 0, XH, XL)
            pe.wait_ge(lfc_in, 16)
            for r in range(16):
                mm = pe.transpose(bank[2 + r // 4][0:FOX_HEADS, (r % 4) * P:(r % 4 + 1) * P],
                                  cp_raw[:, r * FOX_HEADS:(r + 1) * FOX_HEADS], idf[:, :])
                if r % 4 == 3:
                    mm.then_inc(cp_pe, 1)
            block(Lin(1), 1, XH, XL)
            pe.wait_ge(ff_lf, 1)
            pe.wait_ge(col_sb, 1)
            for t in range(NT):
                mm = pe.transpose(bank[6][:, t * 8:t * 8 + 8], lfT[0:FOX_HEADS, tok(t)], idf[0:FOX_HEADS, 0:FOX_HEADS])
            mm.then_inc(lfn_pe, 1)
            block(Lin(2), 0, XH, XL)
            pe.wait_ge(ff_c, 1)
            for t in range(NT):
                mm = pe.transpose(bank[7][:, t * 8:t * 8 + 8], cT[0:FOX_HEADS, tok(t)], idf[0:FOX_HEADS, 0:FOX_HEADS])
            mm.then_inc(cn_pe, 1)
            block(Lin(3), 1, XH, XL)

            pe.wait_ge(consts, 5)
            pe.wait_ge(cn_sb, 1)

            def fox_window(a, par, proj):
                b = a * 3 + (B_FOX + 3)
                s = (B_FOX + 3 + par) % 2
                some = bool(a.terms) or a.c > 0

                def turn_kc(j):
                    if j == 0:
                        pe.wait_ge(head_in[par], (a.half() * 80 + 80).v)
                        if some:
                            pe.wait_ge(kv_copied, (a * 3).v)
                    if j >= 2:
                        pe.wait_ge(kc_copied, (a * 4 + (j - 1)).v)
                    for i in range(4):
                        mm = pe.transpose(TBK[j % 2][:, i * P:(i + 1) * P], KC[par][:, 4 * j + i, :], idf[:, :])
                    mm.then_inc(kc_turned, 1)

                def turn_kv(j):
                    if j < 2:
                        pe.wait_ge(kc_copied, (a * 4 + (3 + j)).v)
                    if j == 2:
                        pe.wait_ge(kv_copied, (a * 3 + 1).v)
                    for i in range(4 * j, min(4 * j + 4, 2 * NT)):
                        src = VTt if i < NT else KTt
                        mm = pe.transpose(TBK[j % 2][:, (i - 4 * j) * P:(i - 4 * j + 1) * P], src[:, par, tok(i % NT)], idf[:, :])
                    mm.then_inc(kv_turned, 1)

                def scores(p):
                    t, S = ORD[p], SBK[p % 2]
                    if p == 0:
                        pe.wait_ge(z_free[0], b.v)
                        pe.wait_ge(z_free[1], b.v)
                    if p < 2:
                        if some:
                            pe.wait_ge(s_read, (a * 5).v)
                            if p == 1:
                                pe.wait_ge(y_done, (a * 5).v)
                    else:
                        pe.wait_ge(s_read, (a * 5 + (p - 1)).v)
                    w, mask = (t + 1) * P, mask_p
                    if t == NTP:
                        pe.wait_ge(qb_ready, (a + 1).v)
                        pe.wait_ge(kc_copied, (a * 4 + 4).v)
                        for i in range(NB):
                            pe.matmul(S[:, 0:PAST], QB[:, i, :], KCT[:, 2 * i:2 * i + 2, :].rearrange("p a b -> p (a b)"),
                                      start=(i == 0), stop=(i == NB - 1))
                        w, mask = PAST + P, mask_s
                        pe.matmul(S[:, PAST:w], QT[:, par, TP:T], KTt[:, par, TP:T], start=True, stop=False)
                    else:
                        pe.matmul(S[:, 0:w], QT[:, par, tok(t)], KTt[:, par, 0:w], start=True, stop=False)
                    pe.matmul(S[:, w - P:w], idb[:, :], mask[:, :], start=False, stop=True).then_inc(s_done, 1)

                def turn_p(p):
                    t = ORD[p]
                    n = t + 1 if t < NTP else 3
                    pe.wait_ge(p_normed, (a * 5 + (p + 1)).v)
                    if some or p > 0:
                        pe.wait_ge(p_copied, (a * 5 + p).v)
                    for i in range(n):
                        mm = pe.transpose(TBK[2][:, i * P:(i + 1) * P], SP[:, p % 2, i * P:(i + 1) * P], idf[:, :])
                    mm.then_inc(p_turned, 1)

                def times_v(p):
                    t = ORD[p]
                    pe.wait_ge(p_copied, (a * 5 + (p + 1)).v)
                    pe.wait_ge(kv_copied, (a * 3 + min(p + 1, 3) if p else a * 3 + 1).v)
                    if p < 4 and (some or p > 0):
                        pe.wait_ge(y_done, (a * 5 + p).v)
                    if p == 4:
                        pe.wait_ge(s_read, (a * 5 + 4).v)
                    pt, O = PTB[:, p % 2, :], OB[p]
                    if t < NTP:
                        for i in range(t + 1):
                            mm = pe.matmul(O[:, 0:P], KVN[:, i, :], pt[:, i * P:(i + 1) * P], start=(i == 0), stop=(i == t))
                    else:
                        pe.matmul(O[:, 0:P], KVN[:, NTP, :], pt[:, 0:P], start=True, stop=False)
                        for i in range(NB):
                            for f in range(2):
                                mm = pe.matmul(O[:, 0:P], VC[par][:, 2 * i + f, :], PM[:, f, i, :], start=False,
                                               stop=(i == NB - 1 and f == 1))
                    mm.then_inc(o_done, 1)

                def unit(*todo):
                    def run():
                        for f, x in todo:
                            f(x)
                    return run

                u = [unit((turn_kc, 0), (turn_kc, 1), (scores, 0), (scores, 1)),
                     unit((turn_kc, 2), (turn_kc, 3), (turn_p, 0), (turn_kv, 0)),
                     unit((scores, 2), (turn_p, 1), (times_v, 0), (turn_kv, 1), (turn_kv, 2)),
                     unit((scores, 3), (turn_p, 2), (times_v, 1)),
                     unit((scores, 4), (turn_p, 3), (times_v, 2)),
                     unit((turn_p, 4), (times_v, 3), (times_v, 4))]
                if proj:
                    block(b, s, XH, XL, (u[0], u[1]))
                    block(b + 1, 1 - s, XH, XL, (u[2], u[3]))
                    block(b + 2, s, XH, XL, (u[4], u[5]))
                else:
                    merge_begin(0, (u[0], u[1]), (u[2], u[3]))
                    u[4]()
                    u[5]()

            def merge_begin(r, after0=(None, None), after1=(None, None)):
                block(Lin(B_MG[r]), B_MG[r] % 2, XH, XL, after0)
                block(Lin(B_MG[r] + 1), (B_MG[r] + 1) % 2, XH, XL, after1)

            fox_window(Lin(0), 0, True)
            with pe.Fori(0, FOX_HEADS // 2 - 1) as i:
                fox_window(Lin(1, (2, i)), 1, True)
                fox_window(Lin(2, (2, i)), 0, True)
            fox_window(Lin(FOX_HEADS - 1), 1, False)

            def merge(r, y_sem, y_count):
                s = B_MG[r] % 2
                pe.wait_ge(y_sem, y_count)
                with pe.Fori(0, KT // 2 - 1) as i:
                    for q in range(2):
                        b = Lin(B_MG[r] + 2 + 2 * q, (4, i))
                        block(b, s, YH, YL)
                        block(b + 1, 1 - s, XH, XL)
                for q in range(2):
                    block(Lin(B_MG[r] + 2 * KT - 2 + q), (s + q) % 2, YH, YL)

            merge(0, y_done, 5 * FOX_HEADS)

            def lru_gates(n):
                pe.wait_ge(xc_ready, (n + 1).v)
                pe.wait_ge(wg_in, (n * 32 + 32).v)
                if n.terms or n.c > 0:
                    pe.wait_ge(r_act, n.v)
                for i in range(2):
                    for h in range(2):
                        mm = pe.matmul(bank[2 + 2 * i + h][:, 0:HT], WG[:, i, :], XC[:, h * HT:(h + 1) * HT],
                                       start=True, stop=True)
                mm.then_inc(g_mm, 1)

            def lru_window(n, lag):
                b = n * 2 + B_LRU
                block(b, B_LRU % 2, XH, XL, ((lambda: lru_gates(n + -1)) if lag else None, None))
                block(b + 1, 1 - B_LRU % 2, XH, XL)

            lru_window(Lin(0), False)
            with pe.Fori(0, LRU_N - 1) as i:
                lru_window(Lin(1, (1, i)), True)
            merge_begin(1, (lambda: lru_gates(Lin(LRU_N - 1)), None))
            pe.wait_ge(r_act, LRU_N)
            pe.wait_ge(last_dve, 1)
            for n in range(LRU_N):
                mm = pe.transpose(bank[2 + n // 4][0:36, (n % 4) * P:(n % 4 + 1) * P], last[:, n, :], idf[:, :])
            mm.then_inc(last_pe, 1)
            merge(1, yl_done, LRU_N)

            def turn_o(h):
                pe.wait_ge(go_ready, (h + 1).v)
                pe.wait_ge(ds_read, (h * 8 + 8).v)
                for t in range(NT):
                    for e in range(2):
                        mm = pe.transpose(TBK[t // 2][:, (2 * (t % 2) + e) * P:(2 * (t % 2) + e + 1) * P],
                                          OS[:, t, e * P:(e + 1) * P], idf[:, :])
                mm.then_inc(gt_turned, 1)

            def gla_head(h):
                b = h * 6 + B_GLA
                s = B_GLA % 2
                some = bool(h.terms) or h.c > 0

                def gate():
                    if some:
                        turn_o(h + -1)
                    pe.wait_ge(gu_in, (h * 16 + 16).v)
                    if some:
                        pe.wait_ge(ds_read, (h * 8).v)
                        pe.wait_ge(at_ready, (h * 2).v)
                    else:
                        pe.wait_ge(last_sb, 1)
                    for q in range(2):
                        mm = pe.matmul(SBK[q][:, 0:HT], GU[0:GLA_RANK, :], glr[:, q * HT:(q + 1) * HT], start=True, stop=True)
                    mm.then_inc(gg_mm, 1)

                def turn_ke():
                    pe.wait_ge(ke_ready, (h + 1).v)
                    if some:
                        pe.wait_ge(gt_copied, (h * 3).v)
                    for t in range(NT):
                        mm = pe.transpose(TBK[t // 4][:, (t % 4) * P:(t % 4 + 1) * P], KG[:, tok(t)], idf[:, :])
                    mm.then_inc(ke_turned, 1)

                def turn_v():
                    pe.wait_ge(z_free[0], (b + 3).v)
                    pe.wait_ge(z_free[1], (b + 3).v)
                    pe.wait_ge(ken_ready, (h + 1).v)
                    for t in range(NT):
                        for e in range(2):
                            at = (2 * (t % 2) + e) * P
                            mm = pe.transpose(TBK[t // 2][:, at:at + P], VT2[:, e, tok(t)], idf[:, :])
                    mm.then_inc(v_turned, 1)

                def states(places, todo):
                    for bk, pair in places:
                        for q, i in enumerate(pair):
                            w, x = todo(i)
                            mm = pe.matmul(bank[bk][:, q * GLA_DV:(q + 1) * GLA_DV], w, x, start=True, stop=True)
                        mm.then_inc(ds_done, 1)

                def state_prompt():
                    def part(i):
                        rows = slice((i % 2) * GLA_CH, (i % 2 + 1) * GLA_CH)
                        return KEN[rows, i // 2, :], VN[rows, i // 2, :]
                    pe.wait_ge(v_copied, (h + 1).v)
                    states(DS_PROMPT, part)

                def state_sample():
                    pe.wait_ge(kem_ready, (h + 1).v)
                    pe.wait_ge(ds_read, (h * 8 + 4).v)
                    pe.wait_ge(at_ready, (h * 2 + 2).v)
                    states(DS_SAMPLE, lambda i: (KEM[:, i, :], VN[:, NTP, :]))

                def scores():
                    pe.wait_ge(q_ready, (h + 1).v)
                    for t in range(NT):
                        if t == 0:
                            pe.wait_ge(ds_read, (h * 8 + 4).v)
                        mm = pe.matmul(SBK[t // 4][:, (t % 4) * P:(t % 4 + 1) * P], KTl[:, tok(t)], QG[:, tok(t)],
                                       start=True, stop=True)
                        if t >= 3:
                            mm.then_inc(at_done, 1)

                def out(t):
                    O = (TBK[2], OBK)[t % 2]
                    if t == NTP:
                        pe.wait_ge(s0_in, (h * 16 + 16).v)
                    pe.wait_ge(at_ready, (h * 2 + (1 if t < NTP else 2)).v)
                    if t >= 2:
                        pe.wait_ge(go_read, (h * 5 + (t - 1)).v)
                    if t < NTP:
                        pe.matmul(O[:, 0:GLA_DV], AT[:, t, :], VN[:, t, :], start=True, stop=False)
                        for c in range(2):
                            mm = pe.matmul(O[c * GLA_CH:(c + 1) * GLA_CH, 0:GLA_DV], QG[:, t * P + c * GLA_CH:t * P + (c + 1) * GLA_CH],
                                           SA[:, 2 * t + c, :], start=False, stop=True)
                    else:
                        pe.matmul(O[:, 0:GLA_DV], AT[:, t, :], VN[:, t, :], start=True, stop=False)
                        for i in range(NB):
                            mm = pe.matmul(O[:, 0:GLA_DV], QGB[:, i, :], S0[:, i, :], start=False, stop=(i == NB - 1))
                    mm.then_inc(go_done, 1)

                def out_tiles():
                    for t in range(NT):
                        out(t)

                block(b, s, XH, XL, (gate, None))
                block(b + 1, 1 - s, XH, XL)
                block(b + 2, s, XH, XL, (None, turn_ke))
                block(b + 3, 1 - s, XH, XL, (turn_v, state_prompt))
                block(b + 4, s, XH, XL, (None, scores))
                block(b + 5, 1 - s, XH, XL, (out_tiles, state_sample))

            gla_head(Lin(0))
            with pe.Fori(0, GLA_H - 1) as i:
                gla_head(Lin(1, (1, i)))
            merge_begin(2, (lambda: turn_o(Lin(GLA_H - 1)), None))
            merge(2, gy_done, 2 * GLA_H)

            def pairs(b0, n, AH, AL, a_ready=None):
                with pe.Fori(0, n) as i:
                    for s in range(2):
                        block(b0.loop(2, i) + s, (b0.c + s) % 2, AH, AL, a_ready=a_ready)
            block(Lin(B_OUT), B_OUT % 2, YH, YL, a_ready=lambda h, k: pe.wait_ge(mix_split, k + 1) if h == 0 else None)
            block(Lin(B_OUT + 1), (B_OUT + 1) % 2, YH, YL)
            pairs(Lin(B_OUT + 2), KT // 2 - 1, YH, YL)

            def natural(n, t):
                c = n * NT + t
                if t >= 2:
                    pe.wait_ge(nat_free, c - 1)
                for k in range(KT):
                    mm = pe.transpose(bank[2 + 2 * (t % 2) + k // 4][:, (k % 4) * P:(k % 4 + 1) * P],
                                      (OTB, MIX)[n][:, k, tok(t)], idf[:, :])
                mm.then_inc(nat_pe, 1)

            for h in range(2):
                pe.wait_ge(z_free[h], B_MLP)
            for t in range(NT + 2):
                if t < NT:
                    natural(0, t)
                if t >= 2:
                    norm_turn(1, t - 2, HS1)
            pe.wait_ge(nt_free, 2 * NT + 2 * (HT // P + 1))

            def group(g):
                b = g * (2 * KT) + B_MLP
                pairs(b, KT // 2, XH, XL, lambda h, k: pe.wait_ge(nt_free, 4 * NT) if (h, k) == (1, 0) else None)

                def u_ready(h, k):
                    if h == 0 and k == 0:
                        pe.wait_ge(u_done[0], (g * KT + KT).v)
                        pe.wait_ge(u_done[1], (g * KT + KT).v)
                    if (h, k) in ((0, KT - 1), (1, 0)):
                        pe.wait_ge(u_done[h], (g * KT + (KT + 1)).v)
                block(b + KT, b.c % 2, YH, YL, a_ready=u_ready)
                block(b + (KT + 1), (b.c + 1) % 2, YH, YL)
                pairs(b + (KT + 2), KT // 2 - 1, YH, YL)

            with pe.Fori(0, NG - 1) as g:
                group(Lin(0, (1, g)))
            group(Lin(NG - 1))
            for h in range(2):
                pe.wait_ge(z_free[h], N_BLK)
            for t in range(NT):
                natural(1, t)

        @blk.gpsimd
        def _(pool):
            step = Steps(pool, pool_step)
            pool.memset(raw[0][:, :, :], 0.0).then_inc(pad_zero, 1)
            pool.memset(vrow[:, :], 0.0).then_inc(pad_zero, 1)
            step(pool.memset(idf[:, :], 0.0))
            pool.affine_select(out=idf[:, :], in_=idf[:, :], compare_op=ALU.not_equal, fill=1.0, base=0,
                               pattern=[[-1, P]], channel_multiplier=1).then_inc(consts, 1)
            pool.wait_ge(consts, 1)
            pool.tensor_copy(idb[:, :], idf[:, :]).then_inc(consts, 1)

            def blocks(m):
                return m[:, :].rearrange("p (b t) -> p b t", t=TS_)
            step(pool.memset(mask_p[:, :], 0.0))
            step(pool.affine_select(out=mask_p[:, :], in_=mask_p[:, :], compare_op=ALU.is_ge, fill=NEG, base=0,
                                    pattern=[[-1, P]], channel_multiplier=1))
            pool.affine_select(out=blocks(mask_s), in_=blocks(mask_p), compare_op=ALU.is_ge, fill=NEG, base=TS_ - 1,
                               pattern=[[TS_, NB], [0, TS_]], channel_multiplier=-1).then_inc(consts, 1)
            step(pool.memset(gmask_s[:, :], 1.0))
            step(pool.affine_select(out=gmask_s[:, :], in_=gmask_s[:, :], compare_op=ALU.is_ge, fill=0.0, base=0,
                                    pattern=[[1, P]], channel_multiplier=-1))
            pool.affine_select(out=gmask_p[:, :].rearrange("p (b t) -> p b t", t=GLA_CH),
                               in_=gmask_s[:, :].rearrange("p (b t) -> p b t", t=GLA_CH), compare_op=ALU.is_ge,
                               fill=0.0, base=0, pattern=[[-GLA_CH, P // GLA_CH], [0, GLA_CH]],
                               channel_multiplier=1).then_inc(consts, 1)
            pool.wait_ge(consts, 4)
            step(pool.affine_select(out=blocks(gmask_s), in_=blocks(gmask_s), compare_op=ALU.is_ge, fill=0.0, base=0,
                                    pattern=[[-TS_, NB], [0, TS_]], channel_multiplier=1))
            step(pool.memset(bmask[:, :], 1.0))
            step(pool.affine_select(out=bmask[:, :], in_=bmask[:, :], compare_op=ALU.is_ge, fill=0.0, base=0,
                                    pattern=[[-TS_, NB]], channel_multiplier=1))
            pool.affine_select(out=bmask[:, :], in_=bmask[:, :], compare_op=ALU.is_ge, fill=0.0, base=TS_ - 1,
                               pattern=[[TS_, NB]], channel_multiplier=-1).then_inc(consts, 1)
            pool.wait_ge(yl_done, LRU_N)
            pool.wait_ge(stored, 32 + 64)
            pool.memset(QGB[:, :, :], 0.0)
            pool.memset(SA[:, 0, :], 0.0)
            step(pool.memset(RG[:, :], 1.0))
            pool.memset(RG[:, 0:TP].rearrange("p (a b) -> p a b", b=GLA_CH)[:, :, 0:1], 0.0)
            pool.memset(by_sample(RG)[:, :, 0:1], 0.0).then_inc(gla_init, 1)
            for t in range(NT - 1):
                pool.wait_ge(nat_free, t + 1)
                pool.tensor_tensor(X2[:, t, :], X2[:, t, :], TM[:, t % 2, :], ALU.add).then_inc(x2_ready, 1)
            pool.wait_ge(x2_root, NT)
            pool.wait_ge(nt_done, 4 * NT)
            pool.memset(MIX[:, :, :], 0.0).then_inc(mlp_zero, 1)
            for t in (0, 2):
                pool.wait_ge(nat_free, NT + t + 1)
                pool.tensor_tensor(X2[:, t, :], X2[:, t, :], FN[:, 0, :], ALU.add).then_inc(fin_pool, 1)

        SS, ROOT, RINV, LAM, LMIN, MX, NMX, RSUM, RSI = range(9)

        def one(v):
            while len(v.shape) > 2:
                v = v.rearrange("p a b -> p (a b)") if len(v.shape) == 3 else v.rearrange("p a b c -> p (a b) c")
            return v

        def at(n):
            return n.ds() if n.terms else slice(n.c, n.c + 1)

        @blk.scalar
        def _(act):
            step = Steps(act, act_step)

            def hi(b, s):
                act.wait_ge(raw_in[s], (b.half() * 16 + 16).v)
                if b.terms or b.c >= 2:
                    act.wait_ge(z_done[1], (b + -1).v)
                act.copy(WH[s][:, :, :], raw[s][:, :, :]).then_inc(w_hi, 1)

            def evac(b, h, dst, scale=1.0):
                act.wait_ge(z_done[h], (b + 1).v)
                act.activation(dst, Z[h][:, 0:HT], ACT.Copy, scale=scale).then_inc(z_free[h], 1)

            def norm_hi(n, t):
                for q in range(2):
                    c = 2 * (n * NT + t) + q
                    act.wait_ge(nt_done, c + 1)
                    act.copy(XH[:, 4 * q:4 * q + 4, tok(t)],
                             bank[(2 + 2 * (t % 2) if n == 0 else 6) + q].rearrange("p (k t) -> p k t", t=P)).then_inc(nt_hi, 1)

            def root_table():
                step(act.activation(small[:, ROOT, 7:8], eps[:, :], ACT.Sqrt))

            def root(src, junk_, t, sig):
                step(act.activation(junk_, src, ACT.Square, accum_out=small[:, SS, t:t + 1]))
                act.activation(small[:, ROOT, t:t + 1], small[:, SS, t:t + 1], ACT.Sqrt, scale=1.0 / D,
                               bias=eps[:, :]).then_inc(sig, 1)

            act.wait_ge(eps_set, 1)
            root_table()
            for t in range(NT + 1):
                if t < NT:
                    act.wait_ge(x_in[t], 16)
                    root(XN[:, t, :], junk[:, :], t, root_done)
                if t == NT - 1:
                    act.wait_ge(pad_in, 16)
                    hi(Lin(0), 0)
                if t >= 1:
                    norm_hi(0, t - 1)
            hi(Lin(1), 1)
            act.wait_ge(col_pe, 1)
            act.copy(col[:, :, :], bank[6][:, 0:KT * NR].rearrange("p (k r) -> p k r", r=NR)).then_inc(col_sb, 1)
            act.wait_ge(col_sb, 1)
            lam = small[:, LAM, :]
            step(act.activation(lam, col[:, :, R_LAM], ACT.Abs))
            step(act.activation(lam, lam, ACT.Exp, scale=-1.0))
            act.activation(lam, lam, ACT.Ln, bias=1.0).then_inc(lam_ln, 1)
            act.wait_ge(vec_in, 16 * 10)
            for h in range(2):
                act.wait_ge(z_done[h], 1)
                step(act.activation(fz[0:FOX_HEADS, h * HT:(h + 1) * HT], Z[h][0:FOX_HEADS, 0:HT], ACT.Identity, bias=bcol[:, :]))
                act.copy(glr[:, h * HT:(h + 1) * HT], Z[h][32:32 + GLA_RANK, 0:HT]).then_inc(z_free[h], 1)
            hi(Lin(2), 0)
            lf8, fz8 = lfT[0:FOX_HEADS, :], fz[0:FOX_HEADS, :]
            step(act.activation(lf8, fz8, ACT.Abs))
            step(act.activation(lf8, lf8, ACT.Exp, scale=-1.0))
            act.activation(lf8, lf8, ACT.Ln, bias=1.0).then_inc(ff_ln, 1)
            for part, dst in enumerate((QT, KTt, VTt)):
                b = B_FOX + part
                if part > 0:
                    hi(Lin(b + 1), (b + 1) % 2)
                for h in range(2):
                    evac(Lin(b), h, dst[:, 0, h * HT:(h + 1) * HT], FOX_DH ** -0.5 if part == 0 else 1.0)

            def gate(r, j, b, s, h):
                act.wait_ge(z_done[h], (b + 1).v)
                if j.terms or j.c >= 2:
                    act.wait_ge(mix_sum, (j + (r * KT - 1)).v)
                act.activation(GT[:, s, h * HT:(h + 1) * HT], Z[h][:, 0:HT], ACT.Tanh, scale=0.5).then_inc(z_free[h], 1)

            def fox_window(a, par, proj):
                b = a * 3 + (B_FOX + 3)
                s = (B_FOX + 3 + par) % 2

                def take(part, h):
                    if not proj:
                        if part < 2:
                            gate(0, Lin(part), b + part, part, h)
                    else:
                        evac(b + part, h, (QT, KTt, VTt)[part][:, 1 - par, h * HT:(h + 1) * HT],
                             FOX_DH ** -0.5 if part == 0 else 1.0)

                def exps(p):
                    t = ORD[p]
                    w = (t + 1) * P if t < NTP else PAST + P
                    act.wait_ge(m_ready, (a * 5 + (p + 1)).v)
                    act.activation(SP[:, p % 2, 0:w], SP[:, p % 2, 0:w], ACT.Exp, bias=small[:, NMX, p:p + 1],
                                   accum_out=small[:, RSUM, p:p + 1]).then_inc(p_ready, 1)

                def kv(j):
                    n = min(4, 2 * NT - 4 * j)
                    act.wait_ge(kv_turned, (a * 3 + (j + 1)).v)
                    if j == 0 and (a.terms or a.c > 0):
                        act.wait_ge(kv_stored, (a * 64).v)
                    act.copy(KVN[:, 4 * j:4 * j + n, :], TBK[j % 2][:, 0:n * P].rearrange("p (t d) -> p t d", d=P)).then_inc(kv_copied, 1)

                def y(p):
                    act.wait_ge(o_done, (a * 5 + (p + 1)).v)
                    act.copy(YH[:, at(a), tok(ORD[p])], OB[p][:, 0:P].unsqueeze(1)).then_inc(y_hi, 1)

                hi(b + 1, 1 - s)
                take(0, 0)
                exps(0)
                exps(1)
                take(0, 1)
                kv(0)
                hi(b + 2, s)
                take(1, 0)
                exps(2)
                y(0)
                kv(1)
                kv(2)
                take(1, 1)
                exps(3)
                y(1)
                take(2, 0)
                if proj:
                    hi(b + 3, 1 - s)
                exps(4)
                y(2)
                take(2, 1)
                y(3)
                y(4)

            fox_window(Lin(0), 0, True)
            with step.loop(FOX_HEADS // 2 - 1, 0) as i:
                fox_window(Lin(1, (2, i)), 1, True)
                fox_window(Lin(2, (2, i)), 0, True)
            fox_window(Lin(FOX_HEADS - 1), 1, False)

            def merge(r):
                b0 = B_MG[r]
                s = b0 % 2
                with step.loop(KT // 2 - 1, 0) as i:
                    for q in range(2):
                        b = Lin(b0 + 2 + 2 * q, (4, i))
                        hi(b + 1, 1 - s)
                        hi(b + 2, s)
                        for h in range(2):
                            gate(r, Lin(2 + q, (2, i)), b + 1, q, h)
                hi(Lin(b0 + 2 * KT - 1), 1 - s)
                hi(Lin(b0 + 2 * KT), s)

            merge(0)

            def lru_window(n, cur, lag):
                b = n * 2 + B_LRU
                s = B_LRU % 2
                m = n + -1
                if not lag:
                    hi(b + 1, 1 - s)
                if cur:
                    if lag:
                        act.wait_ge(xc_ready, n.v)
                    act.wait_ge(z_done[0], (b + 1).v)
                    act.copy(XP[:, 3:3 + HT], Z[0][:, 0:HT]).then_inc(z_free[0], 1)
                else:
                    gate(1, Lin(0), b, 0, 0)
                if lag:
                    act.wait_ge(ge_dve, n.v)
                    act.activation(TG[:, :], GQ[:, :], ACT.Tanh, scale=GELU_A).then_inc(ge_act, 1)
                    act.wait_ge(g_mm, n.v)
                    act.wait_ge(lru_cols, 1)
                    for dst, bk, r, done in ((RX, 4, R_BX, rx_act), (RA, 2, R_BA, r_act)):
                        for h in range(2):
                            ins_ = act.activation(dst[:, h * HT:(h + 1) * HT], bank[bk + h][:, 0:HT], ACT.Tanh, scale=0.5,
                                                  bias=one(col[:, at(m), r:r + 1]))
                        ins_.then_inc(done, 1)
                    act.wait_ge(r_act, n.v)
                    c4, c4n = one(lru_c4[:, 0:1, at(m)]), one(lru_c4[:, 1:2, at(m)])
                    act.activation(TH[:, :], RA[:, :], ACT.Tanh, scale=c4n, bias=c4n)
                if cur:
                    act.wait_ge(z_done[1], (b + 1).v)
                    act.copy(XP[:, 3 + HT:3 + TP], Z[1][:, 0:TP - HT])
                    act.copy(XPS[:, :, CONV_W - 1:], Z[1][:, TP - HT:HT].rearrange("p (b t) -> p b t", t=TS_)).then_inc(z_free[1], 1)
                else:
                    gate(1, Lin(0), b, 0, 1)
                hi(b + 2, s)
                if lag:
                    step(act.activation(AA[:, :], RA[:, :], ACT.Exp, scale=c4, bias=c4))
                    act.activation(A2[:, :], AA[:, :], ACT.Square).then_inc(a_act, 1)
                if cur:
                    if lag:
                        act.wait_ge(ge_out, n.v)
                    evac(b + 1, 0, LG[:, 0:HT])
                if lag:
                    act.wait_ge(m_dve, n.v)
                    act.activation(MM[:, :], MM[:, :], ACT.Sqrt).then_inc(m_act, 1)
                if cur:
                    evac(b + 1, 1, LG[:, HT:T])
                    for h in range(2):
                        act.wait_ge(z_free[h], (b + 2).v)
                    act.activation(GQ[:, :], LG[:, :], ACT.Square, scale=GELU_B ** 0.5).then_inc(ge_sq, 1)
                    hi(b + 3, 1 - s)
                if lag:
                    act.wait_ge(h_ready, n.v)
                    act.copy(YH[:, at(m), :], MM[:, :].unsqueeze(1)).then_inc(yl_hi, 1)

            act.wait_ge(y_done, 5 * FOX_HEADS)
            act.wait_ge(kv_stored, 64 * FOX_HEADS)
            lru_window(Lin(0), True, False)
            with step.loop(LRU_N - 1, 1) as i:
                lru_window(Lin(1, (1, i)), True, True)
            lru_window(Lin(LRU_N), False, True)
            for h in range(2):
                gate(1, Lin(1), Lin(B_MG[1] + 1), 1, h)
            act.wait_ge(last_pe, 1)
            act.copy(LS[0:36, :], psum[0:36, 2:4, :].rearrange("p a b -> p (a b)")).then_inc(last_sb, 1)
            merge(1)

            def o_copy(h):
                act.wait_ge(gt_turned, (h + 1).v)
                for j in range(3):
                    n = 2 if j < 2 else 1
                    for e in range(2):
                        src = TBK[j].rearrange("p (t e d) -> p t e d", e=2, d=P)[:, 0:n, e, :]
                        dst = OT[:, e, 2 * j * P:(2 * j + n) * P].rearrange("p (t d) -> p t d", d=P)
                        ins_ = act.activation(dst, src, ACT.Copy, scale=col[:, e, R_GN:R_GN + 1])
                    ins_.then_inc(gt_copied, 1)

            def o_hi(h):
                for e in range(2):
                    act.wait_ge(gy_dve, (h * 2 + (e + 1)).v)
                    act.copy(YH[:, h.ds(1, 2, e) if h.terms else slice(2 * h.c + e, 2 * h.c + e + 1), :],
                             OT[:, e, :].unsqueeze(1)).then_inc(gy_hi, 1)

            def gla_head(h):
                b = h * 6 + B_GLA
                s = B_GLA % 2
                some = bool(h.terms) or h.c > 0

                def half(v, q):
                    return v[:, q * HT:(q + 1) * HT]

                if not some:
                    hi(b + 1, 1 - s)
                evac(b, 0, half(KG, 0))
                if some:
                    o_copy(h + -1)
                act.wait_ge(gg_mm, (h + 1).v)
                if some:
                    act.wait_ge(ds_read, (h * 8).v)
                for q in range(2):
                    ins_ = act.activation(half(ZG, q), SBK[q][:, 0:HT], ACT.Identity, bias=one(col[:, at(h), R_BG:R_BG + 1]))
                step(ins_)
                evac(b, 1, half(KG, 1))
                hi(b + 2, s)
                if some:
                    o_hi(h + -1)
                step(act.activation(E1[:, :], ZG[:, :], ACT.Abs))
                step(act.activation(E1[:, :], E1[:, :], ACT.Exp, scale=-1.0))
                act.activation(E2[:, :], E1[:, :], ACT.Ln, bias=1.0).then_inc(gg_act, 1)
                if some:
                    act.wait_ge(gy_done, (h * 2).v)
                for q in range(2):
                    evac(b + 1, q, half(VT2[:, 0, :], q))
                act.wait_ge(gg_dve, (h + 1).v)
                act.activation(E1[:, :], BC[:, :], ACT.Exp, scale=1.0 / GLA_TAU)
                act.activation(E2[:, :], BC[:, :], ACT.Exp, scale=-1.0 / GLA_TAU)
                act.activation(E3[:, :], E3[:, :], ACT.Exp, scale=1.0 / GLA_TAU).then_inc(ge3_act, 1)
                hi(b + 3, 1 - s)
                for q in range(2):
                    evac(b + 2, q, half(VT2[:, 1, :], q))
                act.wait_ge(ke_turned, (h + 1).v)
                act.wait_ge(ke_ready, (h + 1).v)
                act.copy(KEN[:, 0:4, :], TBK[0].rearrange("p (t d) -> p t d", d=P))
                act.copy(KEN[:, 4, :], TBK[1][:, 0:P]).then_inc(ken_ready, 1)
                hi(b + 4, s)
                evac(b + 3, 0, half(QG, 0), GLA_DK ** -0.5)
                act.wait_ge(v_turned, (h + 1).v)
                for j in range(3):
                    n = 2 if j < 2 else 1
                    ins_ = act.copy(VN[:, 2 * j:2 * j + n, :], TBK[j][:, 0:n * GLA_DV].rearrange("p (t d) -> p t d", d=GLA_DV))
                ins_.then_inc(v_copied, 1)
                evac(b + 3, 1, half(QG, 1), GLA_DK ** -0.5)
                hi(b + 5, 1 - s)
                for e in range(2):
                    if e == 1:
                        hi(b + 6, s)
                    for q in range(2):
                        act.wait_ge(z_done[q], (b + (5 + e)).v)
                        act.activation(half(SG[:, e, :], q), Z[q][:, 0:HT], ACT.Tanh, scale=0.5).then_inc(sg_tanh, 1)
                        if (e, q) == (1, 0):
                            for t in range(NT):
                                O = (TBK[2], OBK)[t % 2]
                                act.wait_ge(go_done, (h * 5 + (t + 1)).v)
                                step(act.copy(OS[:, t, :], O[:, 0:GLA_DV]))
                                act.activation(E2[:, 0:GLA_DV], O[:, 0:GLA_DV], ACT.Square,
                                               accum_out=small[:, SS, t:t + 1]).then_inc(go_read, 1)
                            act.wait_ge(go_read, (h * 5 + 5).v)
                            act.activation(small[:, ROOT, 0:NT], small[:, SS, 0:NT], ACT.Sqrt, scale=1.0 / GLA_DV,
                                           bias=eps[:, :]).then_inc(go_root, 1)
                hi(b + 7, 1 - s)

            act.wait_ge(gla_init, 1)
            act.wait_ge(stored, 32 + 64)
            gla_head(Lin(0))
            with step.loop(GLA_H - 1, 8) as i:
                gla_head(Lin(1, (1, i)))
            gate(2, Lin(0), Lin(B_MG[2]), 0, 0)
            o_copy(Lin(GLA_H - 1))
            o_hi(Lin(GLA_H - 1))
            gate(2, Lin(0), Lin(B_MG[2]), 0, 1)
            hi(Lin(B_MG[2] + 2), B_MG[2] % 2)
            for h in range(2):
                gate(2, Lin(1), Lin(B_MG[2] + 1), 1, h)
            merge(2)

            for h in range(2):
                act.wait_ge(z_done[h], B_OUT)
            for k in range(KT):
                act.wait_ge(mix_sum, 2 * KT + k + 1)
                act.copy(YH[:, k, :], MIX[:, k, :]).then_inc(mix_hi, 1)

            def pairs(b0, n, per, body, n0=Lin(0)):
                with step.loop(n, per) as i:
                    for s in range(2):
                        b = b0.loop(2, i) + s
                        hi(b + 1, (b0.c + s + 1) % 2)
                        body(b, i * 2 + s, n0.loop(2, i) + s)

            def to_otb(b, j, _):
                for h in range(2):
                    evac(b, h, OTB[:, bass.ds(j, 1), h * HT:(h + 1) * HT].rearrange("p a b -> p (a b)"))
            pairs(Lin(B_OUT), KT // 2, 0, to_otb)
            root_table()

            for t in range(NT + 2):
                if t < NT:
                    act.wait_ge(nat_pe, t + 1)
                    root(psum[:, 2 + 2 * (t % 2):4 + 2 * (t % 2), :], NJ[:, :].rearrange("p (a b) -> p a b", b=512), t, nat_root)
                if 1 <= t <= NT:
                    act.wait_ge(*((x2_ready, t) if t < NT else (x2_last, 1)))
                    root(X2[:, t - 1, :], NJ[:, :], t - 1, x2_root)
                if t >= 2:
                    norm_hi(1, t - 2)

            def up(b, j, n):
                for h in range(2):
                    half = slice(h * HT, (h + 1) * HT)
                    act.wait_ge(z_done[h], (b + 1).v)
                    act.wait_ge(u_done[h], (n + 1).v)
                    act.activation(UR[:, half], Z[h][:, 0:HT], ACT.Relu).then_inc(z_free[h], 1)
                    act.wait_ge(z_free[h], (b + 1).v)
                    step(act.activation(UQ[:, half], UR[:, half], ACT.Square))
                    act.copy(YH[:, bass.ds(j, 1), half], UQ[:, half].unsqueeze(1)).then_inc(u_hi, 1)

            def group(g, last=False):
                b = g * (2 * KT) + B_MLP
                pairs(b, KT // 2, 4, up, g * KT)
                pairs(b + KT, KT // 2 - last, 0, lambda *_: None)
                if last:
                    hi(Lin(N_BLK - 1), (N_BLK - 1) % 2)

            with step.loop(NG - 1, 4 * KT // 2) as g:
                group(Lin(0, (1, g)))
            group(Lin(NG - 1), True)
            root_table()
            for t in range(NT):
                act.wait_ge(nat_pe, NT + t + 1)
                root(psum[:, 2 + 2 * (t % 2):4 + 2 * (t % 2), :], FJ[:, :].rearrange("p (a b) -> p a b", b=512), t, nat_root)

        @blk.vector
        def _(dve):
            step = Steps(dve, dve_step)

            def lo(b, s):
                dve.wait_ge(w_hi, (b + 1).v)
                dve.tensor_tensor(WL[s][:, :, :], raw[s][:, :, :], WH[s][:, :, :].bitcast(F32), ALU.subtract).then_inc(w_lo, 1)

            def norm_lo(n, t):
                for q in range(2):
                    c = 2 * (n * NT + t) + q
                    dve.wait_ge(nt_hi, c + 1)
                    dve.tensor_tensor(XL[:, 4 * q:4 * q + 4, tok(t)],
                                      bank[(2 + 2 * (t % 2) if n == 0 else 6) + q].rearrange("p (k t) -> p k t", t=P),
                                      XH[:, 4 * q:4 * q + 4, tok(t)].bitcast(F32), ALU.subtract).then_inc(nt_free, 1)

            def rinv(t, n=1):
                step(dve.reciprocal(small[:, RINV, t:t + n], small[:, ROOT, t:t + n]))

            def normed(n, t, x, g, HS):
                rinv(t)
                if t >= 2:
                    dve.wait_ge(nt_done, 2 * (n * NT + t - 2) + 2)
                dve.scalar_tensor_tensor(out=HS[:, t % 2, :], in0=x, scalar=small[:, RINV, t:t + 1], in1=g,
                                         op0=ALU.mult, op1=ALU.mult).then_inc(hs_done, 1)

            dve.memset(eps[:, :], EPS).then_inc(eps_set, 1)
            dve.memset(rst_p[0:FOX_HEADS, :], 1.0)
            step(dve.memset(rst_n[0:FOX_HEADS, :], 1.0))
            dve.memset(rst_p[0:FOX_HEADS, :].rearrange("p (b s) -> p b s", s=PAST)[:, :, 0:1], 0.0)
            step(dve.memset(by_sample(rst_n[0:FOX_HEADS, :])[:, :, 0:1], 0.0))
            dve.wait_ge(g_rows, 16)
            for t in range(NT + 1):
                if t < NT:
                    dve.wait_ge(root_done, t + 1)
                    normed(0, t, XN[:, t, :], G0[:, :], HS0)
                if t == NT - 1:
                    lo(Lin(0), 0)
                if t >= 1:
                    norm_lo(0, t - 1)
            lo(Lin(1), 1)
            dve.wait_ge(hs_done, NT)
            dve.memset(PM[:, :, :, :], 0.0)
            step(dve.memset(QB[:, :, :], 0.0))
            dve.wait_ge(col_sb, 1)
            step(dve.tensor_scalar(small[:, LMIN, :], col[:, :, R_LAM], 0.0, None, ALU.min))
            dve.tensor_scalar(col[:, :, R_BA:R_BX + 1], col[:, :, R_BA:R_BX + 1], 0.5, None, ALU.mult)
            dve.wait_ge(lam_ln, 1)
            step(dve.tensor_tensor(small[:, LMIN, :], small[:, LMIN, :], small[:, LAM, :], ALU.subtract))
            dve.tensor_scalar(lru_c4[:, 0, :], small[:, LMIN, :], 0.5 * LRU_C, None, ALU.mult)
            dve.tensor_scalar(lru_c4[:, 1, :], small[:, LMIN, :], -0.5 * LRU_C, None, ALU.mult).then_inc(lru_cols, 1)
            cp8, lf8, fz8, c8, nc8, rn8 = (v[0:FOX_HEADS, :] for v in (cpast, lfT, fz, cT, ncT, rst_n))
            for j in range(4):
                dve.wait_ge(cp_pe, j + 1)
                ins_ = dve.tensor_copy(cp8.rearrange("h (q r) -> h r q", r=16)[:, 4 * j:4 * j + 4, :],
                                       bank[2 + j][0:FOX_HEADS, :].rearrange("h (r q) -> h r q", q=P))
            step(ins_)
            step(dve.tensor_tensor_scan(cp8, rst_p[0:FOX_HEADS, :], cp8, 0.0, ALU.mult, ALU.add))
            lo(Lin(2), 0)
            dve.wait_ge(ff_ln, 1)
            dve.scalar_tensor_tensor(out=lf8, in0=fz8, scalar=0.0, in1=lf8, op0=ALU.min, op1=ALU.subtract).then_inc(ff_lf, 1)
            dve.wait_ge(ff_lf, 1)
            step(dve.tensor_copy(c8, lf8))
            step(dve.tensor_tensor(by_sample(c8)[:, :, 0:1], by_sample(c8)[:, :, 0:1],
                                   cp8.rearrange("h (b s) -> h b s", s=PAST)[:, :, PAST - 1:PAST], ALU.add))
            step(dve.tensor_tensor_scan(c8, rn8, c8, 0.0, ALU.mult, ALU.add))
            dve.tensor_scalar(nc8, c8, -1.0, None, ALU.mult).then_inc(ff_c, 1)
            dve.tensor_scalar(cp8, cp8, -1.0, None, ALU.mult).then_inc(cp_scan, 1)
            dve.wait_ge(lfn_pe, 1)
            dve.tensor_copy(lfn[:, :, :], bank[6][:, 0:NT * 8].rearrange("p (t h) -> p t h", h=8)).then_inc(lfn_sb, 1)
            lo(Lin(3), 1)
            dve.wait_ge(cn_pe, 1)
            dve.tensor_copy(cn[:, :, :], bank[7][:, 0:NT * 8].rearrange("p (t h) -> p t h", h=8)).then_inc(cn_sb, 1)
            dve.wait_ge(cn_sb, 1)
            lo(Lin(4), 0)

            def fox_window(a, par, proj):
                b = a * 3 + (B_FOX + 3)
                s = (B_FOX + 3 + par) % 2
                some = bool(a.terms) or a.c > 0

                def kc(j):
                    dve.wait_ge(kc_turned, (a * 4 + (j + 1)).v)
                    dve.tensor_copy(KCT[:, 4 * j:4 * j + 4, :], TBK[j % 2].rearrange("p (t d) -> p t d", d=P)).then_inc(kc_copied, 1)

                def soft(p):
                    t = ORD[p]
                    w, c0 = ((t + 1) * P, 0) if t < NTP else (PAST + P, TP)
                    if p < 2:
                        if some:
                            dve.wait_ge(p_turned, (a * 5).v)
                    else:
                        dve.wait_ge(p_turned, (a * 5 + (p - 1)).v)
                    dve.wait_ge(s_done, (a * 5 + (p + 1)).v)
                    dve.scalar_tensor_tensor(out=SP[:, p % 2, 0:w], in0=SBK[p % 2][:, 0:w], scalar=one(cn[:, t:t + 1, at(a)]),
                                             in1=CB[:, par, c0:c0 + w], op0=ALU.add, op1=ALU.add).then_inc(s_read, 1)
                    dve.wait_ge(s_read, (a * 5 + (p + 1)).v)
                    step(dve.tensor_reduce(small[:, MX, p:p + 1], SP[:, p % 2, 0:w], AX.X, ALU.max))
                    dve.tensor_scalar(small[:, NMX, p:p + 1], small[:, MX, p:p + 1], -1.0, None, ALU.mult).then_inc(m_ready, 1)

                def pt(p):
                    t = ORD[p]
                    dve.wait_ge(p_turned, (a * 5 + (p + 1)).v)
                    if p < 2:
                        if some:
                            dve.wait_ge(o_done, (a * 5).v)
                    else:
                        dve.wait_ge(o_done, (a * 5 + (p - 1)).v)
                    if t < NTP:
                        dve.tensor_copy(PTB[:, p % 2, 0:(t + 1) * P], TBK[2][:, 0:(t + 1) * P]).then_inc(p_copied, 1)
                    else:
                        for f in range(2):
                            dve.tensor_copy(diag(PM[:, f, :, :]), TBK[2][:, f * P:(f + 1) * P].rearrange("p (b t) -> p b t", t=TS_))
                        dve.tensor_copy(PTB[:, p % 2, 0:P], TBK[2][:, 2 * P:3 * P]).then_inc(p_copied, 1)

                def norm(p):
                    t = ORD[p]
                    w = (t + 1) * P if t < NTP else PAST + P
                    dve.wait_ge(p_ready, (a * 5 + (p + 1)).v)
                    step(dve.reciprocal(small[:, RSI, p:p + 1], small[:, RSUM, p:p + 1]))
                    dve.tensor_scalar(SP[:, p % 2, 0:w], SP[:, p % 2, 0:w], small[:, RSI, p:p + 1], None,
                                      ALU.mult).then_inc(p_normed, 1)

                def y(p):
                    dve.wait_ge(y_hi, (a * 5 + (p + 1)).v)
                    dve.tensor_tensor(YL[:, at(a), tok(ORD[p])], OB[p][:, 0:P].unsqueeze(1),
                                      YH[:, at(a), tok(ORD[p])].bitcast(F32), ALU.subtract).then_inc(y_done, 1)

                lo(b + 1, 1 - s)
                dve.wait_ge(z_free[0], b.v)
                dve.wait_ge(z_free[1], b.v)
                if some:
                    dve.wait_ge(s_done, (a * 5).v)
                dve.tensor_copy(diag(QB), QT[:, par, TP:T].rearrange("p (b t) -> p b t", t=TS_)).then_inc(qb_ready, 1)
                kc(0)
                kc(1)
                dve.wait_ge(head_in[par], (a.half() * 80 + 80).v)
                soft(0)
                soft(1)
                norm(0)
                kc(2)
                kc(3)
                pt(0)
                norm(1)
                lo(b + 2, s)
                soft(2)
                pt(1)
                y(0)
                norm(2)
                soft(3)
                pt(2)
                y(1)
                norm(3)
                soft(4)
                pt(3)
                if proj:
                    lo(b + 3, 1 - s)
                y(2)
                norm(4)
                pt(4)
                y(3)
                y(4)

            fox_window(Lin(0), 0, True)
            with step.loop(FOX_HEADS // 2 - 1, 20) as i:
                fox_window(Lin(1, (2, i)), 1, True)
                fox_window(Lin(2, (2, i)), 0, True)
            fox_window(Lin(FOX_HEADS - 1), 1, False)

            def merge(r):
                b0 = B_MG[r]
                s = b0 % 2

                def add(b, j, q):
                    for h in range(2):
                        half = slice(h * HT, (h + 1) * HT)
                        m = one(MIX[:, j, half])
                        g = GT[:, q, half]
                        dve.wait_ge(z_done[h], (b + 1).v)
                        dve.scalar_tensor_tensor(out=g, in0=g, scalar=1.0, in1=Z[h][:, 0:HT],
                                                 op0=ALU.add, op1=ALU.mult).then_inc(z_free[h], 1)
                        dve.wait_ge(z_free[h], (b + 1).v)
                        if r == 0:
                            ins_ = dve.tensor_scalar(m, g, 0.5, None, ALU.mult)
                        else:
                            ins_ = dve.scalar_tensor_tensor(out=m, in0=g, scalar=0.5, in1=m, op0=ALU.mult, op1=ALU.add)
                        if h == 0:
                            step(ins_)
                        else:
                            ins_.then_inc(mix_sum, 1)

                with step.loop(KT // 2 - 1, 2) as i:
                    for q in range(2):
                        b = Lin(b0 + 2 + 2 * q, (4, i))
                        lo(b + 1, 1 - s)
                        add(b, bass.ds(i * 2 + q, 1), q)
                        lo(b + 2, s)
                for q in range(2):
                    b = Lin(b0 + 2 * KT - 2 + q)
                    lo(b + 1, (b.c + 1) % 2)
                    add(b, slice(KT - 2 + q, KT - 1 + q), q)

            merge(0)

            def lru_window(n, cur, lag):
                b = n * 2 + B_LRU
                s = B_LRU % 2
                m = n + -1
                if not lag:
                    lo(b + 1, 1 - s)
                else:
                    dve.wait_ge(ge_act, n.v)
                    dve.scalar_tensor_tensor(out=Y2[:, :], in0=TG[:, :], scalar=1.0, in1=LG[:, :], op0=ALU.add,
                                             op1=ALU.mult).then_inc(ge_out, 1)
                    dve.wait_ge(ge_out, n.v)
                    dve.wait_ge(rx_act, n.v)
                    step(dve.scalar_tensor_tensor(out=UU[:, :], in0=RX[:, :], scalar=1.0, in1=XC[:, :], op0=ALU.add, op1=ALU.mult))
                lo(b + 2, s)
                if lag:
                    dve.wait_ge(a_act, n.v)
                    dve.scalar_tensor_tensor(out=MM[:, :], in0=A2[:, :], scalar=1.0, in1=TH[:, :], op0=ALU.add,
                                             op1=ALU.mult).then_inc(m_dve, 1)
                if cur:
                    for h in range(2):
                        dve.wait_ge(z_free[h], (b + 1).v)
                    step.mark(dve.tensor_copy(XPS[:, :, 0:3], col[:, at(n), R_CONV0:R_CONV0 + 24].rearrange("p o (b j) -> p (o b) j", j=3)))
                    for j in range(CONV_W):
                        w = one(col[:, at(n), R_CW + j:R_CW + j + 1])
                        for part, (src, dst) in enumerate(((XP[:, j:j + TP], XC[:, 0:TP]), (XPS[:, :, j:j + TS_], by_sample(XC)))):
                            if j > 0 or part == 1:
                                step.wait(but=0 if (j, part) == (CONV_W - 1, 1) else 1)
                            if j == 0:
                                ins_ = dve.tensor_scalar(dst, src, w, one(col[:, at(n), R_CB:R_CB + 1]), ALU.mult, ALU.add)
                            else:
                                ins_ = dve.scalar_tensor_tensor(out=dst, in0=src, scalar=w, in1=dst, op0=ALU.mult, op1=ALU.add)
                            if j < CONV_W - 1:
                                step.mark(ins_)
                    dve.tensor_copy(last[:, at(n), 0:3], XP[:, TP:TP + 3].unsqueeze(1))
                    dve.tensor_copy(last[:, at(n), 3:27].rearrange("p o (b j) -> p (o b) j", j=3), XPS[:, :, TS_:]).then_inc(xc_ready, 1)
                if lag:
                    dve.wait_ge(m_act, n.v)
                    step(dve.scalar_tensor_tensor(out=UU[:, :], in0=UU[:, :], scalar=0.5, in1=MM[:, :], op0=ALU.mult, op1=ALU.mult))
                    h0 = col[:, at(m), R_H0:R_H0 + NB].rearrange("p a b -> p (a b)").unsqueeze(2)
                    first_a, first_u = by_sample(AA)[:, :, 0:1], by_sample(UU)[:, :, 0:1]
                    step(dve.tensor_tensor(fix[:, :, :], first_a, h0, ALU.mult))
                    step(dve.tensor_tensor(first_u, first_u, fix[:, :, :], ALU.add))
                    step(dve.memset(first_a, 0.0))
                    step(dve.tensor_tensor_scan(HH[:, :], AA[:, :], UU[:, :], 0.0, ALU.mult, ALU.add))
                    dve.scalar_tensor_tensor(out=MM[:, :], in0=Y2[:, :], scalar=0.5, in1=HH[:, :], op0=ALU.mult,
                                             op1=ALU.mult).then_inc(h_ready, 1)
                    dve.tensor_copy(last[:, at(m), 27:28], HH[:, TP - 1:TP].unsqueeze(1))
                    step(dve.tensor_copy(last[:, at(m), 28:36], by_sample(HH)[:, :, TS_ - 1:TS_].rearrange("p b o -> p o b")))
                if cur:
                    dve.wait_ge(ge_sq, (n + 1).v)
                    dve.scalar_tensor_tensor(out=GQ[:, :], in0=GQ[:, :], scalar=1.0, in1=LG[:, :], op0=ALU.add,
                                             op1=ALU.mult).then_inc(ge_dve, 1)
                    lo(b + 3, 1 - s)
                if lag:
                    dve.wait_ge(yl_hi, n.v)
                    dve.tensor_tensor(YL[:, at(m), :], MM[:, :].unsqueeze(1), YH[:, at(m), :].bitcast(F32),
                                      ALU.subtract).then_inc(yl_done, 1)

            step(dve.memset(XP[:, 0:CONV_W - 1], 0.0))
            lru_window(Lin(0), True, False)
            with step.loop(LRU_N - 1, 14) as i:
                lru_window(Lin(1, (1, i)), True, True)
            lru_window(Lin(LRU_N), False, True)
            dve.memset(fix[:, :, :], 0.0).then_inc(last_dve, 1)
            merge(1)

            def o_gated(h):
                dve.wait_ge(gt_copied, (h * 3 + 3).v)
                for e in range(2):
                    dve.scalar_tensor_tensor(out=OT[:, e, :], in0=SG[:, e, :], scalar=0.5, in1=OT[:, e, :], op0=ALU.mult,
                                             op1=ALU.mult).then_inc(gy_dve, 1)

            def o_lo(h):
                for e in range(2):
                    dve.wait_ge(gy_hi, (h * 2 + (e + 1)).v)
                    j = h.ds(1, 2, e) if h.terms else slice(2 * h.c + e, 2 * h.c + e + 1)
                    dve.tensor_tensor(YL[:, j, :], OT[:, e, :].unsqueeze(1), YH[:, j, :].bitcast(F32),
                                      ALU.subtract).then_inc(gy_done, 1)

            def gla_head(h):
                b = h * 6 + B_GLA
                s = B_GLA % 2

                def half(v, q):
                    return v[:, q * HT:(q + 1) * HT]

                def silu(e, q):
                    dve.wait_ge(sg_tanh, (h * 4 + (2 * e + q + 1)).v)
                    v = half(SG[:, e, :], q)
                    dve.scalar_tensor_tensor(out=v, in0=v, scalar=1.0, in1=Z[q][:, 0:HT], op0=ALU.add,
                                             op1=ALU.mult).then_inc(z_free[q], 1)

                def add_state(i, places, dec, S, nxt, signal):
                    bk, q = next((bk, pair.index(i)) for bk, pair in places if i in pair)
                    ins_ = dve.scalar_tensor_tensor(out=S[:, nxt, :], in0=S[:, i, :], scalar=E1[:, dec:dec + 1],
                                                    in1=bank[bk][:, q * GLA_DV:(q + 1) * GLA_DV], op0=ALU.mult, op1=ALU.add)
                    if signal:
                        ins_.then_inc(ds_read, 1)
                    else:
                        step(ins_)

                if not (h.terms or h.c > 0):
                    lo(b + 1, 1 - s)
                else:
                    o_gated(h + -1)
                lo(b + 2, s)
                if h.terms or h.c > 0:
                    o_lo(h + -1)
                dve.wait_ge(gg_act, (h + 1).v)
                step(dve.scalar_tensor_tensor(out=ZG[:, :], in0=ZG[:, :], scalar=0.0, in1=E2[:, :], op0=ALU.min, op1=ALU.subtract))
                step(dve.tensor_tensor_scan(BC[:, :], RG[:, :], ZG[:, :], 0.0, ALU.mult, ALU.add))
                for lo_, hi_, c in ((0, TP, GLA_CH), (TP, T, TS_)):
                    v, d = (w[:, lo_:hi_].rearrange("p (a b) -> p a b", b=c) for w in (BC, E3))
                    ins_ = dve.tensor_tensor(d, v[:, :, c - 1:c].broadcast_to((P, (hi_ - lo_) // c, c)), v, ALU.subtract)
                ins_.then_inc(gg_dve, 1)
                dve.wait_ge(ge3_act, (h + 1).v)
                for q in range(2):
                    dve.wait_ge(z_free[q], (b + 1).v)
                step(dve.tensor_tensor(KTl[:, :], KG[:, :], E2[:, :], ALU.mult))
                dve.tensor_tensor(KG[:, :], KG[:, :], E3[:, :], ALU.mult).then_inc(ke_ready, 1)
                lo(b + 3, 1 - s)
                dve.wait_ge(ken_ready, (h + 1).v)
                dve.tensor_tensor(KEM[:, :, :], KEN[:, NTP, :].unsqueeze(1).broadcast_to((P, NB, P)),
                                  bmask[:, :].unsqueeze(2).broadcast_to((P, NB, P)), ALU.mult).then_inc(kem_ready, 1)
                lo(b + 4, s)
                lo(b + 5, 1 - s)
                for q in range(2):
                    dve.wait_ge(z_free[q], (b + 4).v)
                step(dve.tensor_tensor(QG[:, :], QG[:, :], E1[:, :], ALU.mult))
                dve.tensor_copy(diag(QGB), by_sample(QG)).then_inc(q_ready, 1)
                for i in range(TP // GLA_CH):
                    if i % 4 == 0:
                        dve.wait_ge(ds_done, (h * 8 + (i // 2 + 2)).v)
                    if i > 0 and i % 2 == 0:
                        dve.wait_ge(ds_read, (h * 8 + (i // 2)).v)
                    add_state(i, DS_PROMPT, i * GLA_CH + GLA_CH - 1, SA, i + 1, i % 2 == 1)
                silu(0, 0)
                silu(0, 1)
                dve.wait_ge(at_done, (h * 2 + 1).v)
                dve.tensor_tensor(AT[:, 0:4, :], SBK[0].rearrange("p (t s) -> p t s", s=P),
                                  gmask_p[:, :].unsqueeze(1).broadcast_to((P, 4, P)), ALU.mult).then_inc(at_ready, 1)
                dve.wait_ge(at_done, (h * 2 + 2).v)
                dve.tensor_tensor(AT[:, 4, :], SBK[1][:, 0:P], gmask_s[:, :], ALU.mult).then_inc(at_ready, 1)
                lo(b + 6, s)
                silu(1, 0)
                dve.wait_ge(go_root, (h + 1).v)
                rinv(0, NT)
                for t in range(NT):
                    ins_ = dve.tensor_scalar(OS[:, t, :], OS[:, t, :], small[:, RINV, t:t + 1], None, ALU.mult)
                ins_.then_inc(go_ready, 1)
                silu(1, 1)
                dve.wait_ge(go_done, (h * 5 + 5).v)
                for i in range(NB):
                    if i % 2 == 0:
                        dve.wait_ge(ds_done, (h * 8 + (i // 2 + 5)).v)
                    add_state(i, DS_SAMPLE, TP + i * TS_ + TS_ - 1, S0, i, i % 2 == 1)
                lo(b + 7, 1 - s)

            dve.wait_ge(gla_init, 1)
            gla_head(Lin(0))
            with step.loop(GLA_H - 1, 13) as i:
                gla_head(Lin(1, (1, i)))
            o_gated(Lin(GLA_H - 1))
            o_lo(Lin(GLA_H - 1))
            lo(Lin(B_MG[2] + 2), B_MG[2] % 2)
            merge(2)

            for k in range(KT):
                dve.wait_ge(mix_hi, k + 1)
                dve.tensor_tensor(YL[:, k, :], MIX[:, k, :], YH[:, k, :].bitcast(F32), ALU.subtract).then_inc(mix_split, 1)

            def pairs(b0, n, per, body):
                with step.loop(n, per) as i:
                    for s in range(2):
                        b = b0.loop(2, i) + s
                        lo(b + 1, (b0.c + s + 1) % 2)
                        body(b, i * 2 + s)
            pairs(Lin(B_OUT), KT // 2, 0, lambda *_: None)

            def out_normed(n, t, g, tmp):
                dve.wait_ge(nat_root, n * NT + t + 1)
                rinv(t)
                src = psum[:, 2 + 2 * (t % 2):4 + 2 * (t % 2), :]
                dve.scalar_tensor_tensor(out=tmp.rearrange("p (a b) -> p a b", b=512), in0=src, scalar=small[:, RINV, t:t + 1],
                                         in1=g[:, :].rearrange("p (a b) -> p a b", b=512), op0=ALU.mult, op1=ALU.mult).then_inc(nat_free, 1)

            dve.wait_ge(x_again, 16 * 5)
            for t in range(NT + 2):
                if t < NT:
                    if t >= 2:
                        dve.wait_ge(x2_ready, t - 1)
                    out_normed(0, t, G1, TM[:, t % 2, :])
                if t == NT - 1:
                    dve.wait_ge(nat_free, NT)
                    dve.tensor_tensor(X2[:, NT - 1, :], X2[:, NT - 1, :], TM[:, (NT - 1) % 2, :], ALU.add).then_inc(x2_last, 1)
                if 1 <= t <= NT:
                    dve.wait_ge(x2_root, t)
                    normed(1, t - 1, X2[:, t - 1, :], G2[:, :], HS1)
                if t >= 2:
                    norm_lo(1, t - 2)

            for h in range(2):
                dve.memset(fix[:, h:h + 1, :], 0.0).then_inc(u_done[h], 1)

            def group(g, last=False):
                b = g * (2 * KT) + B_MLP
                up_hi = g * (2 * KT)

                with step.loop(KT // 2, 0) as i:
                    for s in range(2):
                        lo(b.loop(2, i) + (s + 1), (b.c + s + 1) % 2)
                        for h in range(2):
                            half = slice(h * HT, (h + 1) * HT)
                            dve.wait_ge(u_hi, (up_hi.loop(4, i) + (2 * s + h + 1)).v)
                            dve.tensor_tensor(YL[:, bass.ds(i * 2 + s, 1), half], UQ[:, half].unsqueeze(1),
                                              YH[:, bass.ds(i * 2 + s, 1), half].bitcast(F32), ALU.subtract).then_inc(u_done[h], 1)

                def down(b, j):
                    for h in range(2):
                        half = slice(h * HT, (h + 1) * HT)
                        m = MIX[:, j, half]
                        if len(m.shape) > 2:
                            m = m.rearrange("p a b -> p (a b)")
                        dve.wait_ge(mlp_zero, 1)
                        dve.wait_ge(z_done[h], (b + 1).v)
                        dve.tensor_tensor(m, m, Z[h][:, 0:HT], ALU.add).then_inc(z_free[h], 1)

                with step.loop(KT // 2 - last, 0) as i:
                    for s in range(2):
                        bb = (b + KT).loop(2, i) + s
                        lo(bb + 1, (b.c + s + 1) % 2)
                        down(bb, bass.ds(i * 2 + s, 1))
                if last:
                    lo(Lin(N_BLK - 1), (N_BLK - 1) % 2)
                    down(Lin(N_BLK - 2), KT - 2)
                    down(Lin(N_BLK - 1), KT - 1)

            with step.loop(NG - 1, 0) as g:
                group(Lin(0, (1, g)))
            group(Lin(NG - 1), True)
            for t in range(NT):
                if t in (2, 4):
                    dve.wait_ge(fin_pool, t // 2)
                out_normed(1, t, G3, FN[:, t % 2, :])
                if t not in (0, 2):
                    dve.wait_ge(nat_free, NT + t + 1)
                    dve.tensor_tensor(X2[:, t, :], X2[:, t, :], FN[:, t % 2, :], ALU.add).then_inc(fin_dve, 1)


_INS = ['x_prompt', 'x_sample', 'cache_fox_k', 'cache_fox_v', 'cache_fox_logf', 'state_lru_conv', 'state_lru_h',
        'state_gla', 'norm_mix_pre', 'norm_mix_post', 'w_in', 'b_fox_f', 'lru_conv_w', 'lru_conv_b', 'lru_w_a',
        'lru_b_a', 'lru_w_x', 'lru_b_x', 'lru_lambda', 'gla_w_gate_up', 'gla_b_gate', 'gla_norm', 'w_branch',
        'w_out', 'norm_mlp_pre', 'norm_mlp_post', 'w_up', 'w_down']
_OUTS = [(1, 512, 1024), (8, 16, 1024), (1, 1, 512, 8, 128), (1, 1, 512, 8, 128), (1, 1, 512, 8), (1, 1, 3, 1024),
         (1, 1, 1024), (1, 1, 4, 128, 256), (1, 8, 16, 8, 128), (1, 8, 16, 8, 128), (1, 8, 16, 8), (1, 8, 3, 1024),
         (1, 8, 1024), (1, 8, 4, 128, 256)]


def kernel(**inputs):
    import numpy as _np
    import concourse.bacc as _bacc
    from concourse import mybir as _mybir
    from concourse.bass_utils import run_bass_kernel_spmd as _run

    nc = _bacc.Bacc("TRN2", target_bir_lowering=False, num_devices=1)
    arrays, ins, outs = {}, [], []
    for name in _INS:
        a = _np.ascontiguousarray(inputs[name])
        arrays[f"in_{name}_dram"] = a
        ins.append(nc.dram_tensor(f"in_{name}_dram", a.shape, _mybir.dt.from_np(a.dtype), kind="ExternalInput").ap())
    for i, shape in enumerate(_OUTS):
        outs.append(nc.dram_tensor(f"out_{i}_dram", shape, F32, kind="ExternalOutput").ap())
    build(nc, ins, outs)
    r = _run(nc, [arrays], core_ids=[0])
    return tuple(r.results[0][f"out_{i}_dram"] for i in range(len(_OUTS)))
```
